# Optimizing a Trainium2 kernel written in Bass

```python
import jax
import jax.numpy as jnp
from jax import lax
import numpy as np

D_MODEL = 1024
BATCH = 1
SEQ = 256
DEPTH = 2

N_MIXERS = 2
MLA_HEADS = 8
MLA_Q_RANK = 256
MLA_KV_RANK = 256
MLA_NOPE = 128
MLA_ROPE = 64
MLA_V = 128
ROPE_THETA = 10000.0
Q_BLOCK = 128
MAX_POS_OFFSET = 2048
MLSTM_PF = 2
MLSTM_INNER = MLSTM_PF * D_MODEL
MLSTM_HEADS = 4
MLSTM_HD = MLSTM_INNER // MLSTM_HEADS
MLSTM_CONV = 4
MLSTM_QKV_BLOCK = 4
MLSTM_CHUNK = 64
N_EXPERTS = 16
N_GROUPS = 4
EXPERTS_PER_GROUP = N_EXPERTS // N_GROUPS
TOP_K = 2
EXPERT_FF = 512
DN_ALPHA = (2.0 * DEPTH) ** 0.25
DN_BETA = (8.0 * DEPTH) ** -0.25
LN_EPS = 1e-5
N_MLA_LAYERS = (DEPTH + 1) // 2
N_MLSTM_LAYERS = DEPTH // 2

kernel_name = "hybrid_mla_mlstm_grouped_moe_deepnorm"

def layer_norm(x, g, b):
    xf = x.astype(jnp.float32)
    mu = jnp.mean(xf, axis=-1, keepdims=True)
    var = jnp.mean(jnp.square(xf - mu), axis=-1, keepdims=True)
    return ((xf - mu) * lax.rsqrt(var + LN_EPS) * g.astype(jnp.float32) + b.astype(jnp.float32)).astype(x.dtype)

def rms_norm(x, g):
    xf = x.astype(jnp.float32)
    y = xf * lax.rsqrt(jnp.mean(jnp.square(xf), axis=-1, keepdims=True) + LN_EPS)
    return (y * g.astype(jnp.float32)).astype(x.dtype)

def rope_tables(positions):
    inv_freq = 1.0 / (ROPE_THETA ** (jnp.arange(0, MLA_ROPE, 2, dtype=jnp.float32) / MLA_ROPE))
    ang = positions.astype(jnp.float32)[..., None] * inv_freq
    return jnp.cos(ang), jnp.sin(ang)

def apply_rope(x, cos, sin):
    x1, x2 = jnp.split(x.astype(jnp.float32), 2, axis=-1)
    return jnp.concatenate([x1 * cos - x2 * sin, x1 * sin + x2 * cos], axis=-1).astype(x.dtype)

def mla_mixer(x, cos, sin, w_in, g_q, w_uq, g_kv, w_ukv, w_o):
    B, S, _ = x.shape
    c = x @ w_in
    c_q, c_kv, k_pe = jnp.split(c, [MLA_Q_RANK, MLA_Q_RANK + MLA_KV_RANK], axis=-1)
    q = (rms_norm(c_q, g_q) @ w_uq).reshape(B, S, MLA_HEADS, MLA_NOPE + MLA_ROPE)
    q_nope, q_pe = jnp.split(q, [MLA_NOPE], axis=-1)
    q_pe = apply_rope(q_pe, cos[:, :, None, :], sin[:, :, None, :])
    k_pe = apply_rope(k_pe, cos, sin)
    kv = (rms_norm(c_kv, g_kv) @ w_ukv).reshape(B, S, MLA_HEADS, MLA_NOPE + MLA_V)
    k_nope, v = jnp.split(kv, [MLA_NOPE], axis=-1)
    scale = (MLA_NOPE + MLA_ROPE) ** -0.5
    n_blk = S // Q_BLOCK
    key_idx = jnp.arange(S)

    def one_block(args):
        qn, qp, start = args
        s = jnp.einsum('bqhd,bkhd->bhqk', qn, k_nope) + jnp.einsum('bqhr,bkr->bhqk', qp, k_pe)
        s = s.astype(jnp.float32) * scale
        q_idx = start + jnp.arange(Q_BLOCK)
        s = jnp.where(key_idx[None, :] <= q_idx[:, None], s, -jnp.inf)
        p = jax.nn.softmax(s, axis=-1).astype(v.dtype)
        return jnp.einsum('bhqk,bkhd->bqhd', p, v)

    qn_b = jnp.moveaxis(q_nope.reshape(B, n_blk, Q_BLOCK, MLA_HEADS, MLA_NOPE), 1, 0)
    qp_b = jnp.moveaxis(q_pe.reshape(B, n_blk, Q_BLOCK, MLA_HEADS, MLA_ROPE), 1, 0)
    starts = jnp.arange(n_blk) * Q_BLOCK
    o = lax.map(one_block, (qn_b, qp_b, starts))
    o = jnp.moveaxis(o, 0, 1).reshape(B, S, MLA_HEADS * MLA_V)
    return o @ w_o

def causal_depthwise_conv(x, w, b):
    K, C = w.shape
    y = lax.conv_general_dilated(x, w[:, None, :], window_strides=(1,), padding=[(K - 1, 0)],
                                 dimension_numbers=('NWC', 'WIO', 'NWC'), feature_group_count=C)
    return y + b

def blockdiag_proj(x, w):
    B, S, _ = x.shape
    xb = x.reshape(B, S, w.shape[0], MLSTM_QKV_BLOCK)
    return jnp.einsum('bsgi,gij->bsgj', xb, w).reshape(B, S, -1)

def mlstm_chunkwise(q, k, v, ig, lf):
    B, H, S, DH = q.shape
    L = MLSTM_CHUNK
    nc = S // L
    q = q.astype(jnp.float32)
    k = k.astype(jnp.float32) * (DH ** -0.5)
    v = v.astype(jnp.float32)

    def chunks(a):
        return jnp.moveaxis(a.reshape((B, H, nc, L) + a.shape[3:]), 2, 0)

    causal = jnp.tril(jnp.ones((L, L), dtype=bool))

    def step(carry, inp):
        C, n, m = carry
        qi, ki, vi, igi, lfi = inp
        b = jnp.cumsum(lfi, axis=-1)
        d = jnp.where(causal, b[..., :, None] - b[..., None, :] + igi[..., None, :], -jnp.inf)
        inter = b + m[..., None]
        m_i = jnp.maximum(inter, jnp.max(d, axis=-1))
        w_intra = jnp.exp(d - m_i[..., None])
        w_inter = jnp.exp(inter - m_i)
        s = jnp.einsum('bhid,bhjd->bhij', qi, ki) * w_intra
        num = jnp.einsum('bhij,bhje->bhie', s, vi) + w_inter[..., None] * jnp.einsum('bhid,bhde->bhie', qi, C)
        den = jnp.sum(s, axis=-1) + w_inter * jnp.einsum('bhid,bhd->bhi', qi, n)
        h = num / jnp.maximum(jnp.abs(den), jnp.exp(-m_i))[..., None]
        b_last = b[..., -1]
        g = b_last[..., None] - b + igi
        m_new = jnp.maximum(b_last + m, jnp.max(g, axis=-1))
        w_state = jnp.exp(g - m_new[..., None])
        decay = jnp.exp(b_last + m - m_new)
        C_new = decay[..., None, None] * C + jnp.einsum('bhj,bhjd,bhje->bhde', w_state, ki, vi)
        n_new = decay[..., None] * n + jnp.einsum('bhj,bhjd->bhd', w_state, ki)
        return (C_new, n_new, m_new), h

    init = (jnp.zeros((B, H, DH, DH), jnp.float32), jnp.zeros((B, H, DH), jnp.float32),
            jnp.zeros((B, H), jnp.float32))
    _, h = lax.scan(step, init, (chunks(q), chunks(k), chunks(v), chunks(ig), chunks(lf)))
    return jnp.moveaxis(h, 0, 2).reshape(B, H, S, DH)

def mlstm_mixer(x, w_in, conv_w, conv_b, w_q, w_k, w_v, w_ig, b_ig, w_fg, b_fg, g_out, skip, w_out):
    B, S, _ = x.shape
    xm, z = jnp.split(x @ w_in, 2, axis=-1)
    xc = jax.nn.silu(causal_depthwise_conv(xm, conv_w, conv_b))
    q = blockdiag_proj(xc, w_q)
    k = blockdiag_proj(xc, w_k)
    v = blockdiag_proj(xm, w_v)
    qkv = jnp.concatenate([q, k, v], axis=-1)
    ig = (qkv @ w_ig + b_ig).astype(jnp.float32)
    lf = jax.nn.log_sigmoid((qkv @ w_fg + b_fg).astype(jnp.float32))

    def heads(a):
        return a.reshape(B, S, MLSTM_HEADS, MLSTM_HD).transpose(0, 2, 1, 3)

    h = mlstm_chunkwise(heads(q), heads(k), heads(v), ig.transpose(0, 2, 1), lf.transpose(0, 2, 1))
    h = h.transpose(0, 2, 1, 3)
    mu = jnp.mean(h, axis=-1, keepdims=True)
    var = jnp.mean(jnp.square(h - mu), axis=-1, keepdims=True)
    h = ((h - mu) * lax.rsqrt(var + LN_EPS)).reshape(B, S, MLSTM_INNER) * g_out.astype(jnp.float32)
    h = (h.astype(x.dtype) + skip * xc) * jax.nn.silu(z)
    return h @ w_out

def grouped_moe(x, router_w, router_b, w_gate, w_up, w_down):
    B, S, _ = x.shape
    scores = jax.nn.sigmoid((x @ router_w).astype(jnp.float32))
    sel = (scores + router_b.astype(jnp.float32)).reshape(B, S, N_GROUPS, EXPERTS_PER_GROUP)
    top_vals, top_idx = lax.top_k(sel, TOP_K)
    group = jnp.argmax(jnp.sum(top_vals, axis=-1), axis=-1)
    idx = jnp.take_along_axis(top_idx, group[..., None, None], axis=2)[..., 0, :]
    expert_ids = group[..., None] * EXPERTS_PER_GROUP + idx
    w = jnp.take_along_axis(scores, expert_ids, axis=-1)
    w = w / jnp.sum(w, axis=-1, keepdims=True)
    gate = jnp.einsum('bsk,bske->bse', w, jax.nn.one_hot(expert_ids, N_EXPERTS, dtype=jnp.float32)).astype(x.dtype)
    y = jnp.zeros_like(x)
    for e in range(N_EXPERTS):
        h = jax.nn.silu(x @ w_gate[e]) * (x @ w_up[e])
        y = y + gate[..., e:e + 1] * (h @ w_down[e])
    return y

def setup_inputs(seed: int = 0) -> dict:
    key = jax.random.key(seed)
    ks = jax.random.split(key, 32)

    def nrm(k, shape, scale):
        return jax.random.normal(k, shape, jnp.float32) * scale

    nA, nB = N_MLA_LAYERS, N_MLSTM_LAYERS
    qk_dim = MLA_NOPE + MLA_ROPE
    offset = jax.random.randint(ks[1], (BATCH, 1), 0, MAX_POS_OFFSET, dtype=jnp.int32)
    positions = offset + jnp.arange(SEQ, dtype=jnp.int32)[None, :]
    b_fg = jnp.broadcast_to(jnp.linspace(3.0, 6.0, MLSTM_HEADS, dtype=jnp.float32), (nB, MLSTM_HEADS))
    return {
        "x": nrm(ks[0], (BATCH, SEQ, D_MODEL), 1.0),
        "positions": positions,
        "router_w": nrm(ks[2], (D_MODEL, N_EXPERTS), D_MODEL ** -0.5),
        "router_b": nrm(ks[3], (N_EXPERTS,), 0.01),
        "mla_w_in": nrm(ks[4], (nA, D_MODEL, MLA_Q_RANK + MLA_KV_RANK + MLA_ROPE), D_MODEL ** -0.5),
        "mla_g_q": 1.0 + nrm(ks[5], (nA, MLA_Q_RANK), 0.02),
        "mla_w_uq": nrm(ks[6], (nA, MLA_Q_RANK, MLA_HEADS * qk_dim), MLA_Q_RANK ** -0.5),
        "mla_g_kv": 1.0 + nrm(ks[7], (nA, MLA_KV_RANK), 0.02),
        "mla_w_ukv": nrm(ks[8], (nA, MLA_KV_RANK, MLA_HEADS * (MLA_NOPE + MLA_V)), MLA_KV_RANK ** -0.5),
        "mla_w_o": nrm(ks[9], (nA, MLA_HEADS * MLA_V, D_MODEL), DN_BETA * (MLA_HEADS * MLA_V) ** -0.5),
        "mlstm_w_in": nrm(ks[10], (nB, D_MODEL, 2 * MLSTM_INNER), D_MODEL ** -0.5),
        "mlstm_conv_w": nrm(ks[11], (nB, MLSTM_CONV, MLSTM_INNER), MLSTM_CONV ** -0.5),
        "mlstm_conv_b": nrm(ks[12], (nB, MLSTM_INNER), 0.02),
        "mlstm_w_q": nrm(ks[13], (nB, MLSTM_INNER // MLSTM_QKV_BLOCK, MLSTM_QKV_BLOCK, MLSTM_QKV_BLOCK), MLSTM_QKV_BLOCK ** -0.5),
        "mlstm_w_k": nrm(ks[14], (nB, MLSTM_INNER // MLSTM_QKV_BLOCK, MLSTM_QKV_BLOCK, MLSTM_QKV_BLOCK), MLSTM_QKV_BLOCK ** -0.5),
        "mlstm_w_v": nrm(ks[15], (nB, MLSTM_INNER // MLSTM_QKV_BLOCK, MLSTM_QKV_BLOCK, MLSTM_QKV_BLOCK), MLSTM_QKV_BLOCK ** -0.5),
        "mlstm_w_ig": nrm(ks[16], (nB, 3 * MLSTM_INNER, MLSTM_HEADS), 0.1 * (3 * MLSTM_INNER) ** -0.5),
        "mlstm_b_ig": nrm(ks[17], (nB, MLSTM_HEADS), 0.1),
        "mlstm_w_fg": nrm(ks[18], (nB, 3 * MLSTM_INNER, MLSTM_HEADS), 0.1 * (3 * MLSTM_INNER) ** -0.5),
        "mlstm_b_fg": b_fg + nrm(ks[19], (nB, MLSTM_HEADS), 0.1),
        "mlstm_g_out": 1.0 + nrm(ks[20], (nB, MLSTM_INNER), 0.02),
        "mlstm_skip": 1.0 + nrm(ks[21], (nB, MLSTM_INNER), 0.02),
        "mlstm_w_out": nrm(ks[22], (nB, MLSTM_INNER, D_MODEL), DN_BETA * MLSTM_INNER ** -0.5),
        "moe_w_gate": nrm(ks[23], (DEPTH, N_EXPERTS, D_MODEL, EXPERT_FF), D_MODEL ** -0.5),
        "moe_w_up": nrm(ks[24], (DEPTH, N_EXPERTS, D_MODEL, EXPERT_FF), D_MODEL ** -0.5),
        "moe_w_down": nrm(ks[25], (DEPTH, N_EXPERTS, EXPERT_FF, D_MODEL), DN_BETA * EXPERT_FF ** -0.5),
        "ln_g": 1.0 + nrm(ks[26], (DEPTH, 2, D_MODEL), 0.02),
        "ln_b": nrm(ks[27], (DEPTH, 2, D_MODEL), 0.02),
    }

def reference(x, positions, router_w, router_b,
              mla_w_in, mla_g_q, mla_w_uq, mla_g_kv, mla_w_ukv, mla_w_o,
              mlstm_w_in, mlstm_conv_w, mlstm_conv_b, mlstm_w_q, mlstm_w_k, mlstm_w_v,
              mlstm_w_ig, mlstm_b_ig, mlstm_w_fg, mlstm_b_fg, mlstm_g_out, mlstm_skip, mlstm_w_out,
              moe_w_gate, moe_w_up, moe_w_down, ln_g, ln_b):
    cos, sin = rope_tables(positions)
    for i in range(DEPTH):
        j = i // N_MIXERS
        if i % N_MIXERS == 0:
            y = mla_mixer(x, cos, sin, mla_w_in[j], mla_g_q[j], mla_w_uq[j], mla_g_kv[j],
                          mla_w_ukv[j], mla_w_o[j])
        else:
            y = mlstm_mixer(x, mlstm_w_in[j], mlstm_conv_w[j], mlstm_conv_b[j], mlstm_w_q[j],
                            mlstm_w_k[j], mlstm_w_v[j], mlstm_w_ig[j], mlstm_b_ig[j], mlstm_w_fg[j],
                            mlstm_b_fg[j], mlstm_g_out[j], mlstm_skip[j], mlstm_w_out[j])
        x = layer_norm(DN_ALPHA * x + y, ln_g[i, 0], ln_b[i, 0])
        y = grouped_moe(x, router_w, router_b, moe_w_gate[i], moe_w_up[i], moe_w_down[i])
        x = layer_norm(DN_ALPHA * x + y, ln_g[i, 1], ln_b[i, 1])
    return x


_drawn_inputs = setup_inputs


def setup_inputs(seed=0):
    import zlib

    import numpy as np

    out = dict(_drawn_inputs(seed))
    spreads = {}
    factors = {'mla_g_q': 8.0,
     'mla_g_kv': 8.0,
     'mlstm_conv_b': 6.816,
     'mlstm_w_ig': 2.891,
     'mlstm_b_ig': 200.0,
     'mlstm_w_fg': 8.0,
     'mlstm_g_out': 26.599,
     'mlstm_skip': 24.318}
    for name, (base, spread) in spreads.items():
        noise = np.random.default_rng([zlib.crc32(name.encode()), seed]).standard_normal(out[name].shape)
        drawn = base * np.exp(spread * noise) if base else spread * noise
        out[name] = jnp.asarray(drawn.astype(out[name].dtype))
    for name, factor in factors.items():
        out[name] = (out[name] * factor).astype(out[name].dtype)
    return out
```

```python
from contextlib import ExitStack

import concourse.bass as bass
from concourse import mybir

F32 = mybir.dt.float32
BF16 = mybir.dt.bfloat16
I32 = mybir.dt.int32
ALU = mybir.AluOpType
ACT = mybir.ActivationFunctionType
AX = mybir.AxisListType

P = 128
D = 1024
S = 256
TC = S // P
DC = D // P
HEADS = 8
Q_RANK = KV_RANK = 256
RC = Q_RANK // P
ROPE = 64
HALF = ROPE // 2
HEADS_PER_ROPE = P // HALF
SCALE = (128 + ROPE) ** -0.5
INNER = 2048
IC = INNER // P
M_HEADS = 4
CPH = IC // M_HEADS
HD = INNER // M_HEADS
TAPS = 4
BLK = 4
EXPERTS = 16
GROUPS = 4
PER_GROUP = 4
FF = 512
FC = FF // P
PAIRS = EXPERTS // 2
SLOTS = 64
MAX_ROUNDS = S // SLOTS
ALPHA = (2.0 * 2) ** 0.25
EPS = 1e-5
DOUBLINGS = S.bit_length() - 1
FAR = 1024.0
NEG = -1e30

RING = 12
UNIT = 2048
W_IN = 0
W_UQ = W_IN + DC * 576
W_UKV = W_UQ + RC * 1536
W_O = W_UKV + RC * 2048
M_UNITS_IN = IC
M_UNITS = IC + IC // 2

TWO_PI = 6.283185307179586
PI_A = 6.28125
PI_B = 0.0019350051879882812
PI_C = TWO_PI - PI_A - PI_B
MAGIC = 1.5 * 2 ** 23

COL_GQ, COL_GKV, COL_CONVW, COL_CONVB = 0, 2, 4, 4 + TAPS * IC
COL_GOUT = COL_CONVB + IC
COL_SKIP = COL_GOUT + IC
COL_INVF = COL_SKIP + IC
COLS = COL_INVF + 1


class Steps:

    def __init__(self, engine, sem):
        self.engine, self.sem, self.n = engine, sem, 0

    def did(self, instruction):
        self.n += 1
        return instruction.then_inc(self.sem, 1)

    def settle(self):
        self.engine.wait_ge(self.sem, self.n)


def build_trunk(nc, a, out):
    with ExitStack() as ctx:
        sems = {}

        def sem(name):
            if name not in sems:
                sems[name] = ctx.enter_context(nc.semaphore(name))
            return sems[name]

        def sb(name, shape, dt=F32):
            return ctx.enter_context(nc.sbuf_tensor(name, shape, dt))

        bank = [ctx.enter_context(nc.psum_tensor(f"bank{i}", [P, 512], F32)) for i in range(8)]

        ring = sb("ring", [P, RING * UNIT])
        x_tok = sb("x_tok", [P, TC, D])
        xT = sb("xT", [P, DC, S])
        ln_gb = sb("ln_gb", [P, 2, D])
        cols = sb("cols", [P, COLS])
        ident = sb("ident", [P, P])
        ident_bf = sb("ident_bf", [P, P], BF16)
        causal_bf = sb("causal_bf", [P, P], BF16)
        upto = sb("upto", [P, P])
        before = sb("before", [P, P])
        ones = sb("ones", [P, P])
        zeros_bf = sb("zeros_bf", [P, 512], BF16)
        slot_no = sb("slot_no", [P, SLOTS])
        stats = sb("stats", [P, TC, 2, 6])
        mean_var = sb("mean_var", [P, TC, 2])
        rstd = sb("rstd", [P, TC])
        lower = sb("lower", [P, PER_GROUP, PER_GROUP])
        router_b = sb("router_b", [P, EXPERTS])
        router_w = sb("router_w", [P, DC, EXPERTS])
        gate_b = sb("gate_b", [P, 2 * M_HEADS])
        gate_w = sb("gate_w", [P, 3 * IC, 2 * M_HEADS])
        w_blocks = sb("w_blocks", [P, 3, IC, BLK])
        block_mask = sb("block_mask", [P, P // BLK])
        half_pi = sb("half_pi", [P, 1])
        eps = sb("eps", [P, 1])
        head_row = sb("head_row", [M_HEADS, M_HEADS, P])
        extra_pairs_at = sb("extra_pairs_at", [P, 4], I32)

        arena_floats = 20000
        arena = sb("arena", [P, arena_floats])

        class Carve:
            def __init__(self):
                self.at = 0

            def __call__(self, *shape, dt=F32):
                n = 1
                for s in shape:
                    n *= s
                words = n if dt is F32 else (n + 1) // 2
                v = arena[:, self.at:self.at + words]
                self.at += words
                assert self.at <= arena_floats, self.at
                if dt is not F32:
                    v = v.bitcast(dt)
                if len(shape) > 1:
                    names = "abcd"[:len(shape)]
                    v = v.rearrange(f"p ({' '.join(names)}) -> p {' '.join(names)}",
                                    **dict(zip(names, shape)))
                return v

        block = ctx.enter_context(nc.Block())

        class A:
            v = Carve()
            oT = v(HEADS, S)
            ang = v(S)
            turns = v(2, S)
            posf = v(S)
            cos = v(S)
            sin = v(S)
            sq = v(256)
            ss = v(TC, 2)
            rs = v(TC, 2)
            cn = v(TC, 512)
            kr = v(TC, 2, HEADS_PER_ROPE, HALF)
            cqT = v(RC, S)
            ckvT = v(RC, S)
            kpe = v(2, S)
            kpe_of = v(HEADS_PER_ROPE, 2, S)
            rt = v(2, 2, S)
            qpe = v(2, 2, S)
            qn = v(HEADS, S)
            kn = v(HEADS, S)
            val = v(TC, D)
            mx = v(HEADS, 2)
            nm = v(HEADS, 2)
            sm = v(HEADS, 2)
            rc = v(HEADS, 2)
            p = v(2, 384)
            pT = v(2, 384)
            norm = qn.rearrange("p h s -> p (h s)").rearrange("p (t d) -> p t d", t=TC)

        class E:
            v = Carve()
            norm = v(TC, D)
            parts = v(3, TC, D, dt=BF16)
            rest = v(2, TC, D)
            lg = v(TC, EXPERTS)
            sc = v(TC, EXPERTS)
            sel = v(TC, EXPERTS)
            ge = v(TC * GROUPS, PER_GROUP, PER_GROUP)
            gt = v(TC * GROUPS, PER_GROUP, PER_GROUP)
            rank = v(TC, EXPERTS)
            top = v(TC, EXPERTS)
            gsum = v(TC, GROUPS)
            grank = v(TC, GROUPS)
            den = v(TC)
            rden = v(TC)
            gate = v(TC, EXPERTS)
            mask = v(TC, EXPERTS)
            posm = v(TC, EXPERTS)
            tot = v(EXPERTS)
            most = v(1)
            full_rounds = v(MAX_ROUNDS)
            over = v(MAX_ROUNDS)
            nrounds = v(1)
            posm_all = v(TC, MAX_ROUNDS * EXPERTS + 2)
            gate_all = v(TC, MAX_ROUNDS * EXPERTS + 2)
            oh = v(TC, 2, SLOTS, dt=BF16)
            ohg = v(TC, 2, SLOTS)
            gt_sb = v(TC, P)
            xg = v(DC, 2 * SLOTS)
            sg = v(FF)
            h = v(FF)
            hT = v(FC, 2 * SLOTS)
            ye = v(2, FF)

        class M:
            v = Carve()
            sxc = v(IC, S)
            zT = v(IC, S)
            val = v(TC, INNER)
            p = v(M_HEADS, 384)
            pre = v(TC, 2 * M_HEADS)
            fa = v(TC, M_HEADS)
            fb = v(TC, M_HEADS)
            lf = v(TC, M_HEADS)
            b = v(TC, M_HEADS)
            aa = v(TC, M_HEADS)
            mt = v(TC, M_HEADS)
            em = v(TC, M_HEADS)
            dn = v(2)
            dm = v(2)
            rd = v(2)
            st = v(TC, 6)
            mv = v(TC, 2)
            w1 = v(2)
            w2 = v(2)
            later = v.at
            xm = v(4, S + TAPS - 1)
            cv = v(2, S)
            cv2 = v(2, S)
            xc = v(2, S)
            w3 = v(2, 3, P)
            qk = v(2, 2, S)
            vT = v(2, S)
            v.at = later
            hn = v(TC, 2 * HD)
            norm = hn
            mrow = v(2, P + S)
            ar = v(384)
            er = v(384)

        class LN:
            mla = ((6, 7), (0, 1))
            moe = ((0, 1), (2, 3))
            mlstm = ((0, 1), (6, 7))

        LN_BANKS = (LN.mla, LN.moe, LN.mlstm, LN.moe)
        TURN_BANKS = (4, 2)
        LN_NORM = (A.norm, E.norm, M.norm, E.norm)

        win = ring[:, W_IN:W_UQ].rearrange("p (k n) -> p k n", k=DC)
        wuq = ring[:, W_UQ:W_UKV].rearrange("p (k n) -> p k n", k=RC)
        wukv = ring[:, W_UKV:W_O].rearrange("p (k n) -> p k n", k=RC)
        wo = ring[:, W_O:W_O + HEADS * D].rearrange("p (k n) -> p k n", k=HEADS)

        LANDED = ("slot{}_landed", "slot{}_landed_again")
        LANDED_BEFORE = (0, 16 * M_UNITS // RING)

        def extra_pairs(engine, layer):
            return engine.value_load(extra_pairs_at[0:1, layer:layer + 1], min_val=0,
                                     max_val=PAIRS * (MAX_ROUNDS - 1))

        def slot(u):
            return ring[:, u * UNIT:(u + 1) * UNIT]

        PROJ = [("qn", 0), ("qpe", 0), ("qn", 1), ("qpe", 1), ("qn", 2), ("kn", 0), ("qn", 3), ("kn", 1),
                ("kn", 2), ("kn", 3), ("v", 0), ("v", 1), ("v", 2), ("v", 3)]

        @block.sync
        def _(sp):
            def load(dst, src, name):
                sp.dma_start(dst, src).then_inc(sem(name), 16)

            for half in range(2):
                ks = slice(half * DC // 2, (half + 1) * DC // 2)
                load(xT[:, ks, :], a["xT"][:, ks, :], f"xT_in{half}")
                load(win[:, ks, :], a["mla_in"][:, ks, :], f"w_in{half}")
            load(cols[:, :], a["cols"], "cols_in")
            load(A.ang.bitcast(I32), a["positions"].partition_broadcast(P), "pos_in")
            load(wuq, a["mla_uq"], "w_uq_in")
            load(wukv, a["mla_ukv"], "w_ukv_in")
            load(wo, a["mla_o"], "w_o_in")
            load(x_tok[:, :, :], a["x"].rearrange("(c p) d -> p c d", p=P), "x_in")
            load(ln_gb[:, :, :], a["ln"][0].partition_broadcast(P), "ln_gb_in")
            for name, dst, src in (("small", router_w[:, :, :], a["router_w"]),
                                   ("small", router_b[:, :], a["router_b"].partition_broadcast(P)),
                                   ("small", gate_b[:, :], a["gate_b"].partition_broadcast(P)),
                                   ("small", gate_w[:, :, :], a["gate_w"]),
                                   ("small", w_blocks[:, :, :, :], a["w_blocks"])):
                load(dst, src, "small_in")

            def next_ln(n):
                sp.wait_ge(sem("ln_done"), TC * n)
                load(ln_gb[:, :, :], a["ln"][n].partition_broadcast(P), "ln_gb_in")

            def moe(layer, first_free):
                for u in range(RING):
                    first_free(u)
                    load(slot(u), a["moe"][layer, 0, u], LANDED[layer].format(u))
                next_ln(2 * layer + 1)
                sp.wait_ge(sem(f"moe{layer}_rounds"), 1)
                extra = extra_pairs(sp, layer)
                with sp.Fori(0, extra + (PAIRS - 1)) as before_it:
                    for u in range(RING):
                        sp.wait_ge(sem(f"moe{layer}_used"), before_it * RING + (u + 1))
                        sp.dma_start(slot(u), a["moe"][layer, bass.ds((before_it + 1) % PAIRS, 1), u].rearrange("a p n -> (a p) n")
                                     ).then_inc(sem(LANDED[layer].format(u)), 16)
                return extra

            def mla_region_free(u):
                begin, end = u * UNIT, (u + 1) * UNIT
                if begin < W_UQ:
                    sp.wait_ge(sem("c_ready"), 1)
                if end > W_UQ and begin < W_O:
                    sp.wait_ge(sem("proj_made"), len(PROJ))
                if end > W_O and begin < W_O + HEADS * D:
                    sp.wait_ge(sem("y_ready"), 4)

            extra = moe(0, mla_region_free)

            def mlstm_unit_used(u):
                if u < IC // 2:
                    sp.wait_ge(sem("xm_made"), 2 * u + 2)
                elif u < IC:
                    sp.wait_ge(sem("z_made"), 2 * (u - IC // 2) + 2)
                elif u < M_UNITS - 1:
                    sp.wait_ge(sem("out_used"), u - IC + 1)
                else:
                    sp.wait_ge(sem("y_ready"), 8)

            for u in range(M_UNITS):
                if u < RING:
                    sp.wait_ge(sem("moe0_used"), extra * RING + (PAIRS - 1) * RING + u + 1)
                else:
                    mlstm_unit_used(u - RING)
                load(slot(u % RING), a["mlstm"][u], LANDED[1].format(u % RING))
                if u == RING - 1:
                    next_ln(2)

            moe(1, lambda u: mlstm_unit_used(M_UNITS - RING + u))
            for t in range(TC):
                sp.wait_ge(sem("ln_done"), 3 * TC + t + 1)
                sp.dma_start(out.rearrange("(c p) d -> p c d", p=P)[:, t, :], x_tok[:, t, :]
                             ).then_inc(sem("stored"), 16)
            sp.wait_ge(sem("stored"), 16 * TC)

        @block.gpsimd
        def _(pool):
            own = Steps(pool, sem("pool_steps"))

            def select(dst, src, pattern, op, fill, base, mul):
                own.did(nc.gpsimd.affine_select(out=dst, in_=src, pattern=pattern, compare_op=op, fill=fill,
                                                base=base, channel_multiplier=mul))

            own.did(nc.gpsimd.memset(ident[:, :], 0.0))
            own.did(nc.gpsimd.memset(ones[:, :], 1.0))
            own.did(nc.gpsimd.memset(causal_bf[:, :], 0.0))
            own.did(nc.gpsimd.memset(zeros_bf[:, :], 0.0))
            own.did(nc.gpsimd.memset(eps[:, :], EPS))
            own.did(nc.gpsimd.memset(half_pi[:, :], TWO_PI / 4))
            own.did(nc.gpsimd.memset(block_mask[:, :], 1.0))
            own.did(nc.gpsimd.memset(lower[:, :, :], 1.0))
            own.did(nc.gpsimd.memset(head_row[:, :, :], 0.0))
            own.did(nc.gpsimd.memset(A.kpe_of, 0.0))
            own.did(nc.gpsimd.iota(slot_no[:, :], [[1, SLOTS]], base=0, channel_multiplier=0,
                                   allow_small_or_imprecise_dtypes=True))
            own.settle()
            select(ident[:, :], ident[:, :], [[-1, P]], ALU.not_equal, 1.0, 0, 1)
            select(causal_bf[:, :], causal_bf[:, :], [[-1, P]], ALU.is_ge, NEG, 0, 1)
            select(upto[:, :], ones[:, :], [[1, P]], ALU.is_ge, 0.0, 0, -1)
            select(before[:, :], ones[:, :], [[1, P]], ALU.is_gt, 0.0, 0, -1)
            select(block_mask[:, :], block_mask[:, :], [[-BLK, P // BLK]], ALU.is_ge, 0.0, 0, 1)
            select(lower[:, :, :], lower[:, :, :], [[1, PER_GROUP], [-1, PER_GROUP]], ALU.is_gt, 0.0, 0, 0)
            select(head_row[:, :, :], head_row[:, :, :], [[-1, M_HEADS], [0, P]], ALU.not_equal, 1.0, 0, 1)
            own.settle()
            select(block_mask[:, :], block_mask[:, :], [[BLK, P // BLK]], ALU.is_gt, 0.0, BLK, -1)
            nc.gpsimd.tensor_copy(ident_bf[:, :], ident[:, :]).then_inc(sem("consts"), 1)

            pool.wait_ge(sem("kpe_ready"), 1)
            for j in range(HEADS_PER_ROPE):
                rows = slice(j * HALF, (j + 1) * HALF)
                nc.gpsimd.tensor_copy(A.kpe_of[rows, j], A.kpe[rows]).then_inc(sem("kpe_of_ready"), 1)

            def moe(layer):
                s = f"moe{layer}_"
                for t in range(TC):
                    pool.wait_ge(sem("x_part0"), layer * TC + t + 1)
                    nc.gpsimd.tensor_tensor(E.rest[:, 0, t], x_tok[:, t], E.parts[:, 0, t], ALU.subtract
                                            ).then_inc(sem("x_rest0"), 1)
                for t in range(TC):
                    pool.wait_ge(sem("x_part1"), layer * TC + t + 1)
                    nc.gpsimd.tensor_tensor(E.rest[:, 1, t], E.rest[:, 0, t], E.parts[:, 1, t], ALU.subtract
                                            ).then_inc(sem("x_rest1"), 1)

                pool.wait_ge(sem(f"moe{layer}_rounds"), 1)
                extra = extra_pairs(pool, layer)

                def gates_of(g):
                    pool.wait_ge(sem(s + "oh"), g + 1)
                    nc.gpsimd.tensor_tensor(
                        E.ohg, E.oh, E.gate_all[:, :, bass.ds(g * 2, 2)].unsqueeze(3).broadcast_to([P, TC, 2, SLOTS]),
                        ALU.mult).then_inc(sem(s + "ohg"), 1)

                gates_of(0)
                with pool.Fori(1, extra + PAIRS) as g:
                    pool.wait_ge(sem(s + "gates_turned"), g)
                    gates_of(g)

            moe(0)

            pool.wait_ge(sem("ln_done"), 2 * TC)
            pool.wait_ge(sem("small_in"), 16 * 5)
            for c in range(IC):
                if c >= 2:
                    pool.wait_ge(sem("qkv_made"), c - 1)
                made = nc.gpsimd.tensor_tensor(
                    M.w3[:, c % 2].rearrange("p w (g j) -> p w g j", j=BLK),
                    block_mask[:, :].unsqueeze(1).unsqueeze(3).broadcast_to([P, 3, P // BLK, BLK]),
                    w_blocks[:, :, c].unsqueeze(2).broadcast_to([P, 3, P // BLK, BLK]), ALU.mult)
                made.then_inc(sem("w3_made"), 1)
            for h in range(M_HEADS):
                cs = slice(h * CPH, (h + 1) * CPH)
                pool.wait_ge(sem("hT_taken"), (h + 1) * CPH)
                nc.gpsimd.tensor_tensor(M.zT[:, cs], M.sxc[:, cs], M.zT[:, cs], ALU.mult).then_inc(sem("u_ready"), 1)
            moe(1)

        @block.scalar
        def _(act):
            own = Steps(act, sem("act_steps"))

            def rstd_root(n, t):
                act.wait_ge(sem("ln_var"), n * TC + t + 1)
                nc.scalar.activation(rstd[:, t:t + 1], mean_var[:, t, 1:2], ACT.Sqrt, bias=eps[:, :]
                                     ).then_inc(sem("ln_root"), 1)

            def turned_x(n):
                for t in range(TC):
                    act.wait_ge(sem("xT_made"), TC * n + t + 1)
                    for j in range(2):
                        nc.scalar.copy(xT[:, j * 4:j * 4 + 4, t * P:(t + 1) * P],
                                       bank[TURN_BANKS[t] + j][:, :].rearrange("p (k s) -> p k s", k=4)
                                       ).then_inc(sem("xT_ready"), 1)

            act.wait_ge(sem("consts"), 1)
            act.wait_ge(sem("ang_ready"), 1)
            own.did(nc.scalar.activation(A.sin, A.turns[:, 0], ACT.Sin))
            own.did(nc.scalar.activation(A.cos, A.turns[:, 0], ACT.Abs))
            own.settle()
            nc.scalar.activation(A.cos, A.cos, ACT.Sin, scale=-1.0, bias=half_pi[:, :]).then_inc(sem("rope_ready"), 1)
            act.wait_ge(sem("c_ready"), 1)
            for t in range(TC):
                for part in range(2):
                    last = nc.scalar.activation(A.sq, bank[t][:, part * 256:part * 256 + 256], ACT.Square,
                                                accum_out=A.ss[:, t, part:part + 1])
                    own.did(last)
                    own.settle()
            nc.scalar.activation(A.rs, A.ss, ACT.Sqrt, scale=1.0 / Q_RANK, bias=eps[:, :]).then_inc(sem("c_root"), 1)
            act.wait_ge(sem("cT_ready"), 1)
            act.wait_ge(sem("cols_in"), 16)
            for k in range(RC):
                nc.scalar.activation(A.ckvT[:, k], bank[5][:, k * S:(k + 1) * S], ACT.Identity,
                                     scale=cols[:, COL_GKV + k:COL_GKV + k + 1]).then_inc(sem("ckvT_ready"), 1)

            def project_out(i, dst, src):
                act.wait_ge(sem("proj_made"), i + 1)
                nc.scalar.copy(dst, src).then_inc(sem("proj_by_act"), 1)

            for i, (what, j) in enumerate(PROJ):
                if i % 2 == 0:
                    if what == "v":
                        project_out(i, A.val[:, j // 2, (j % 2) * 512:(j % 2) * 512 + 512], bank[i % 4][:, :])
                    else:
                        project_out(i, (A.qn if what == "qn" else A.kn)[:, 2 * j:2 * j + 2],
                                    bank[i % 4][:, :].rearrange("p (a s) -> p a s", a=2))
            for i in range(HEADS + 1):
                if i < HEADS:
                    act.wait_ge(sem("max_ready"), i + 1)
                    if i >= 2:
                        act.wait_ge(sem("p_turned"), i - 1)
                    for b, (lo, hi) in enumerate(((0, 128), (128, 384))):
                        nc.scalar.activation(A.p[:, i % 2, lo:hi], bank[i % 2][:, lo:hi], ACT.Exp, scale=SCALE,
                                             bias=A.nm[:, i, b:b + 1], accum_out=A.sm[:, i, b:b + 1]
                                             ).then_inc(sem("exp_ready"), 1)
                if i >= 1:
                    act.wait_ge(sem("p_turned"), i)
                    if i >= 3:
                        act.wait_ge(sem("o_made"), i - 2)
                    nc.scalar.copy(A.pT[:, (i - 1) % 2], bank[2 + (i - 1) % 2][:, 0:384]).then_inc(sem("pT_ready"), 1)
            for t in range(TC):
                rstd_root(0, t)

            def moe(layer):
                s = f"moe{layer}_"
                ln = 2 * layer + 1
                for t in range(TC):
                    act.wait_ge(sem("ln_done"), 2 * layer * TC + t + 1)
                    nc.scalar.copy(E.parts[:, 0, t], x_tok[:, t]).then_inc(sem("x_part0"), 1)
                turned_x(2 * layer)
                for t in range(TC):
                    act.wait_ge(sem("x_rest0"), layer * TC + t + 1)
                    nc.scalar.copy(E.parts[:, 1, t], E.rest[:, 0, t]).then_inc(sem("x_part1"), 1)
                act.wait_ge(sem("logits"), layer + 1)
                nc.scalar.activation(E.sc, bank[6][:, 0:TC * EXPERTS].rearrange("p (t e) -> p t e", t=TC), ACT.Sigmoid
                                     ).then_inc(sem("scores"), 1)
                for t in range(TC):
                    act.wait_ge(sem("x_rest1"), layer * TC + t + 1)
                    nc.scalar.copy(E.parts[:, 2, t], E.rest[:, 1, t]).then_inc(sem("x_part2"), 1)
                act.wait_ge(sem(f"moe{layer}_rounds"), 1)
                extra = extra_pairs(act, layer)

                def gathered(count):
                    act.wait_ge(sem(s + "gathered"), count)
                    nc.scalar.copy(E.xg[:, 4:8], bank[7][:, :].rearrange("p (k s) -> p k s", k=4)
                                   ).then_inc(sem(s + "xg_by_act"), 1)

                gathered(1)
                with act.Fori(0, extra + PAIRS) as g:
                    act.wait_ge(sem(s + "used"), g * RING + DC)
                    nc.scalar.activation(E.sg, bank[4][:, :], ACT.Silu).then_inc(sem(s + "silu"), 1)
                    gathered(g + 2)
                    act.wait_ge(sem(s + "h_turned"), g + 1)
                    nc.scalar.copy(E.hT, bank[4][:, :].rearrange("p (k s) -> p k s", k=FC)
                                   ).then_inc(sem(s + "hT"), 1)
                    act.wait_ge(sem(s + "used"), g * RING + RING)
                    nc.scalar.copy(E.ye[:, 1], bank[4][:, :]).then_inc(sem(s + "ye1"), 1)
                for t in range(TC):
                    rstd_root(ln, t)

            moe(0)

            turned_x(1)
            for c in range(IC + 1):
                if c < IC:
                    act.wait_ge(sem("xm_made"), c + 1)
                    if c >= 4:
                        act.wait_ge(sem("conv_done"), c - 3)
                        act.wait_ge(sem("qkv_made"), c - 3)
                    if c == 0:
                        act.wait_ge(sem("pads"), 1)
                    nc.scalar.copy(M.xm[:, c % 4, TAPS - 1:], bank[c % 2][:, 0:S]).then_inc(sem("xm_ready"), 1)
                    act.wait_ge(sem("conv_done"), c + 1)
                    if c >= 2:
                        act.wait_ge(sem("qkv_made"), c - 1)
                    own.did(nc.scalar.activation(M.xc[:, c % 2], M.cv[:, c % 2], ACT.Silu))
                    own.settle()
                    nc.scalar.activation(M.sxc[:, c], M.xc[:, c % 2], ACT.Copy,
                                         scale=cols[:, COL_SKIP + c:COL_SKIP + c + 1]).then_inc(sem("xc_ready"), 1)
                if c >= 1:
                    d = c - 1
                    act.wait_ge(sem("qkv_made"), d + 1)
                    if d >= 2:
                        act.wait_ge(sem("scored"), d - 1)
                    nc.scalar.copy(M.val[:, :, d * P:(d + 1) * P],
                                   bank[4 + d % 2][:, 0:S].rearrange("p (t n) -> p t n", t=TC)
                                   ).then_inc(sem("v_ready"), 1)
                    nc.scalar.copy(M.vT[:, d % 2], bank[4 + d % 2][:, S:2 * S]).then_inc(sem("v_ready"), 1)
            def z_silu(c):
                act.wait_ge(sem("z_made"), c + 1)
                nc.scalar.activation(M.zT[:, c], bank[c % 2][:, 0:S], ACT.Silu).then_inc(sem("z_ready"), 1)
            z_silu(0)
            z_silu(1)
            act.wait_ge(sem("pre_ready"), 1)
            own.did(nc.scalar.activation(M.fa, M.pre[:, :, M_HEADS:], ACT.Abs))
            own.settle()
            own.did(nc.scalar.activation(M.fb, M.fa, ACT.Exp, scale=-1.0))
            own.settle()
            nc.scalar.activation(M.fa, M.fb, ACT.Ln, bias=1.0).then_inc(sem("log_ready"), 1)
            for c in range(2, 8):
                z_silu(c)
            act.wait_ge(sem("m_ready"), 1)
            nc.scalar.activation(M.em, M.mt, ACT.Exp, scale=-1.0).then_inc(sem("em_ready"), 1)
            for h in range(M_HEADS):
                act.wait_ge(sem("reach_ready"), h + 1)
                nc.scalar.activation(M.er, M.ar, ACT.Exp, scale=-1.0).then_inc(sem("decay_ready"), 1)
                z_silu(8 + h)
            for c in range(8 + M_HEADS, IC):
                z_silu(c)
            for h in range(M_HEADS):
                act.wait_ge(sem("h_var"), h + 1)
                nc.scalar.activation(M.w1, M.w2, ACT.Sqrt, bias=eps[:, :]).then_inc(sem("h_root"), 1)
            for t in range(TC):
                rstd_root(2, t)
            moe(1)

        @block.vector
        def _(dve):
            own = Steps(dve, sem("dve_steps"))
            V = nc.vector

            def layer_norm(n, t, y_made):
                x, r = x_tok[:, t], LN_NORM[n][:, t]
                if n == 0 and t == 0:
                    dve.wait_ge(sem("x_in"), 16)
                for half in range(2):
                    hs = slice(half * 512, (half + 1) * 512)
                    y_made(t, half)
                    own.did(V.scalar_tensor_tensor(out=r[:, hs], in0=x[:, hs], scalar=ALPHA,
                                                   in1=bank[LN_BANKS[n][t][half]][:, :], op0=ALU.mult, op1=ALU.add))
                    own.settle()
                    own.did(V.bn_stats(stats[:, t, half], r[:, hs]))
                own.settle()
                V.bn_aggr(mean_var[:, t], stats[:, t]).then_inc(sem("ln_var"), 1)
                dve.wait_ge(sem("ln_root"), TC * n + t + 1)
                own.did(V.reciprocal(rstd[:, t:t + 1], rstd[:, t:t + 1]))
                own.settle()
                own.did(V.tensor_scalar(r, r, mean_var[:, t, 0:1], rstd[:, t:t + 1], ALU.subtract, ALU.mult))
                own.settle()
                if t == 0:
                    dve.wait_ge(sem("ln_gb_in"), 16 * (n + 1))
                own.did(V.tensor_tensor(r, r, ln_gb[:, 0], ALU.mult))
                own.settle()
                V.tensor_tensor(x, r, ln_gb[:, 1], ALU.add).then_inc(sem("ln_done"), 1)

            dve.wait_ge(sem("pos_in"), 16)
            dve.wait_ge(sem("cols_in"), 16)
            own.did(V.tensor_copy(A.posf, A.ang.bitcast(I32)))
            own.settle()
            own.did(V.tensor_scalar(A.ang, A.posf, cols[:, COL_INVF:COL_INVF + 1], None, ALU.mult))
            own.settle()
            own.did(V.tensor_scalar(A.turns[:, 0], A.ang, 1.0 / TWO_PI, MAGIC, ALU.mult, ALU.add))
            own.settle()
            own.did(V.tensor_scalar(A.turns[:, 1], A.turns[:, 0], MAGIC, None, ALU.subtract))
            own.settle()
            for part in (PI_A, PI_B, PI_C):
                own.did(V.scalar_tensor_tensor(out=A.ang, in0=A.turns[:, 1], scalar=-part, in1=A.ang,
                                               op0=ALU.mult, op1=ALU.add))
                own.settle()
            V.tensor_scalar(A.turns[:, 0], A.ang, 3.1415925, -3.1415925, ALU.min, ALU.max
                            ).then_inc(sem("ang_ready"), 1)
            dve.wait_ge(sem("c_ready"), 1)
            for t in range(TC):
                own.did(V.tensor_copy(A.kr[:, t], bank[2 + t][:, 0:ROPE].rearrange("p (b f) -> p b f", b=2)
                                      .unsqueeze(2).broadcast_to([P, 2, HEADS_PER_ROPE, HALF])))
            dve.wait_ge(sem("c_root"), 1)
            own.did(V.reciprocal(A.rs, A.rs))
            own.settle()
            for t in range(TC):
                for part in range(2):
                    ch = slice(part * 256, part * 256 + 256)
                    V.tensor_scalar(A.cn[:, t, ch], bank[t][:, ch], A.rs[:, t, part:part + 1], None, ALU.mult
                                    ).then_inc(sem("cn_ready"), 1)
            dve.wait_ge(sem("cT_ready"), 1)
            for k in range(RC):
                V.tensor_scalar(A.cqT[:, k], bank[4][:, k * S:(k + 1) * S], cols[:, COL_GQ + k:COL_GQ + k + 1], None,
                                ALU.mult).then_inc(sem("cqT_ready"), 1)
            dve.wait_ge(sem("rope_ready"), 1)

            def rotate(src):
                ab = src.rearrange("p (b s) -> p b s", b=2)
                own.did(V.tensor_tensor(A.rt[:, 0], ab, A.cos.unsqueeze(1).broadcast_to([P, 2, S]), ALU.mult))
                return V.tensor_tensor(A.rt[:, 1], ab, A.sin.unsqueeze(1).broadcast_to([P, 2, S]), ALU.mult)

            def rotated(dst):
                own.did(V.tensor_tensor(dst[:, 0], A.rt[:, 0, 0], A.rt[:, 1, 1], ALU.subtract))
                return V.tensor_tensor(dst[:, 1], A.rt[:, 0, 1], A.rt[:, 1, 0], ALU.add)

            own.did(rotate(bank[6][:, :]))
            own.settle()
            rotated(A.kpe).then_inc(sem("kpe_ready"), 1)
            dve.wait_ge(sem("kpe_ready"), 1)
            n_by_dve = 0
            for i, (what, j) in enumerate(PROJ):
                if i % 2 == 0:
                    continue
                dve.wait_ge(sem("proj_made"), i + 1)
                n_by_dve += 1
                src = bank[i % 4][:, :]
                if what == "qpe":
                    own.settle()
                    rotate(src).then_inc(sem("proj_by_dve"), 1)
                    dve.wait_ge(sem("proj_by_dve"), n_by_dve)
                    own.settle()
                    rotated(A.qpe[:, j]).then_inc(sem("rotated"), 1)
                    dve.wait_ge(sem("rotated"), j + 1)
                elif what == "v":
                    V.tensor_copy(A.val[:, j // 2, (j % 2) * 512:(j % 2) * 512 + 512], src
                                  ).then_inc(sem("proj_by_dve"), 1)
                else:
                    V.tensor_copy((A.qn if what == "qn" else A.kn)[:, 2 * j:2 * j + 2],
                                  src.rearrange("p (a s) -> p a s", a=2)).then_inc(sem("proj_by_dve"), 1)

            for i in range(HEADS + 2):
                if 1 <= i <= HEADS:
                    h = i - 1
                    dve.wait_ge(sem("exp_ready"), 2 * i)
                    own.did(V.reciprocal(A.rc[:, h], A.sm[:, h]))
                    own.settle()
                    for b, (lo, hi) in enumerate(((0, 128), (128, 384))):
                        V.tensor_scalar(A.p[:, h % 2, lo:hi], A.p[:, h % 2, lo:hi], A.rc[:, h, b:b + 1], None, ALU.mult
                                        ).then_inc(sem("p_ready"), 1)
                if i < HEADS:
                    dve.wait_ge(sem("s_made"), i + 1)
                    for b, (lo, hi) in enumerate(((0, 128), (128, 384))):
                        own.did(V.tensor_reduce(A.mx[:, i, b:b + 1], bank[i % 2][:, lo:hi], AX.X, ALU.max))
                    own.settle()
                    V.tensor_scalar(A.nm[:, i], A.mx[:, i], -SCALE, None, ALU.mult).then_inc(sem("max_ready"), 1)
                if i >= 2:
                    h = i - 2
                    dve.wait_ge(sem("o_made"), h + 1)
                    V.tensor_copy(A.oT[:, h], bank[4 + h % 2][:, 0:S]).then_inc(sem("oT_ready"), 1)

            for t in range(TC):
                layer_norm(0, t, lambda t, half: dve.wait_ge(sem("y_ready"), 2 * t + half + 1))

            def moe(layer):
                s = f"moe{layer}_"
                ln = 2 * layer + 1
                if layer == 0:
                    dve.wait_ge(sem("small_in"), 16 * 5)
                own.did(V.memset(E.posm_all[:, :, MAX_ROUNDS * EXPERTS:], FAR))
                own.did(V.memset(E.gate_all[:, :, MAX_ROUNDS * EXPERTS:], 0.0))
                for r in range(MAX_ROUNDS):
                    own.did(V.memset(E.full_rounds[:, r:r + 1], float(SLOTS * (r + 1)) if r < MAX_ROUNDS - 1 else FAR))
                dve.wait_ge(sem("scores"), layer + 1)
                own.did(V.tensor_tensor(E.sel, E.sc, router_b[:, :].unsqueeze(1).broadcast_to([P, TC, EXPERTS]),
                                        ALU.add))
                own.settle()

                def ranks(values, n, dst):
                    full = [P, n, PER_GROUP, PER_GROUP]
                    vj = values.unsqueeze(3).broadcast_to(full)
                    vk = values.unsqueeze(2).broadcast_to(full)
                    ge, gt = E.ge[:, 0:n], E.gt[:, 0:n]
                    own.did(V.tensor_tensor(ge, vk, vj, ALU.is_ge))
                    own.did(V.tensor_tensor(gt, vk, vj, ALU.is_gt))
                    own.settle()
                    own.did(V.tensor_tensor(ge, ge, gt, ALU.subtract))
                    own.settle()
                    own.did(V.tensor_tensor(ge, ge, lower[:, :, :].unsqueeze(1).broadcast_to(full), ALU.mult))
                    own.settle()
                    own.did(V.tensor_tensor(ge, ge, gt, ALU.add))
                    own.settle()
                    own.did(V.tensor_reduce(dst, ge, AX.X, ALU.add))
                    own.settle()

                def by_group(v):
                    return v.rearrange("p t (g j) -> p (t g) j", j=PER_GROUP)

                ranks(by_group(E.sel), TC * GROUPS, by_group(E.rank))
                own.did(V.tensor_scalar(E.top, E.rank, 1.5, None, ALU.is_lt))
                own.settle()
                own.did(V.tensor_tensor(E.rank, E.top, E.sel, ALU.mult))
                own.settle()
                own.did(V.tensor_reduce(E.gsum.rearrange("p t g -> p (t g)"), by_group(E.rank), AX.X, ALU.add))
                own.settle()
                ranks(E.gsum, TC, E.grank)
                own.did(V.tensor_scalar(E.grank, E.grank, 0.5, None, ALU.is_lt))
                own.settle()
                own.did(V.tensor_tensor(by_group(E.mask), by_group(E.top), E.grank.rearrange("p t g -> p (t g)")
                                        .unsqueeze(2).broadcast_to([P, TC * GROUPS, PER_GROUP]), ALU.mult))
                own.settle()
                V.tensor_tensor(E.gate, E.mask, E.sc, ALU.mult).then_inc(sem("mask_ready"), 1)
                dve.wait_ge(sem("mask_ready"), layer + 1)
                own.did(V.tensor_reduce(E.den, E.gate, AX.X, ALU.add))
                own.settle()
                own.did(V.reciprocal(E.rden, E.den))
                own.settle()
                own.did(V.tensor_tensor(E.gate, E.gate, E.rden.unsqueeze(2).broadcast_to([P, TC, EXPERTS]), ALU.mult))
                own.settle()
                dve.wait_ge(sem("places"), layer + 1)
                places = bank[7][:, 0:TC * EXPERTS].rearrange("p (t e) -> p t e", t=TC)
                own.did(V.scalar_tensor_tensor(out=E.posm, in0=places, scalar=-FAR, in1=E.mask,
                                               op0=ALU.add, op1=ALU.mult))
                own.did(V.tensor_reduce(E.most, bank[7][:, 64:64 + EXPERTS], AX.X, ALU.max))
                own.settle()
                own.did(V.tensor_scalar(E.over, E.full_rounds, E.most, float(PAIRS), ALU.is_lt, ALU.mult))
                for r in range(MAX_ROUNDS):
                    es = slice(r * EXPERTS, (r + 1) * EXPERTS)
                    own.did(V.tensor_scalar(E.posm_all[:, :, es], E.posm, FAR - SLOTS * r, None, ALU.add))
                    own.did(V.tensor_copy(E.gate_all[:, :, es], E.gate))
                own.settle()
                own.did(V.tensor_reduce(E.nrounds, E.over, AX.X, ALU.add))
                own.settle()
                V.tensor_copy(extra_pairs_at[:, layer:layer + 1], E.nrounds).then_inc(sem(f"moe{layer}_rounds"), 1)
                dve.wait_ge(sem(f"moe{layer}_rounds"), 1)
                extra = extra_pairs(dve, layer)

                def gathered(count):
                    dve.wait_ge(sem(s + "gathered"), count)
                    V.tensor_copy(E.xg[:, 0:4], bank[6][:, :].rearrange("p (k s) -> p k s", k=4)
                                  ).then_inc(sem(s + "xg_by_dve"), 1)

                def one_hot(g):
                    V.tensor_tensor(
                        E.oh, slot_no[:, :].unsqueeze(1).unsqueeze(1).broadcast_to([P, TC, 2, SLOTS]),
                        E.posm_all[:, :, bass.ds(g * 2, 2)].unsqueeze(3).broadcast_to([P, TC, 2, SLOTS]),
                        ALU.is_equal).then_inc(sem(s + "oh"), 1)

                one_hot(0)
                gathered(1)
                with dve.Fori(0, extra + PAIRS) as g:
                    dve.wait_ge(sem(s + "gates_turned"), g + 1)
                    V.tensor_copy(E.gt_sb, bank[6][:, 0:S].rearrange("p (t n) -> p t n", t=TC)
                                  ).then_inc(sem(s + "gates"), 1)
                    one_hot(g + 1)
                    dve.wait_ge(sem(s + "silu"), g + 1)
                    V.tensor_tensor(E.h, E.sg, bank[5][:, :], ALU.mult).then_inc(sem(s + "h"), 1)
                    gathered(g + 2)
                    dve.wait_ge(sem(s + "used"), g * RING + DC + 2)
                    V.tensor_copy(E.ye[:, 0], bank[5][:, :]).then_inc(sem(s + "ye0"), 1)
                for t in range(TC):
                    layer_norm(ln, t, lambda t, half: dve.wait_ge(sem(s + "added"), extra * (2 * TC) + PAIRS * 2 * TC))

            moe(0)

            V.memset(M.xm[:, :, 0:TAPS - 1], 0.0).then_inc(sem("pads"), 1)
            for c in range(IC + 1):
                if c < IC:
                    dve.wait_ge(sem("xm_ready"), c + 1)
                    if c >= 2:
                        dve.wait_ge(sem("xc_ready"), c - 1)
                    x = M.xm[:, c % 4]
                    w = COL_CONVW + c * TAPS
                    ping, pong = M.cv2[:, c % 2], M.cv[:, c % 2]
                    own.did(V.tensor_scalar(ping, x[:, 0:S], cols[:, w:w + 1], None, ALU.mult))
                    own.settle()
                    for tap in range(1, TAPS):
                        own.did(V.scalar_tensor_tensor(out=(pong, ping)[(tap + 1) % 2] if tap < TAPS - 1 else pong,
                                                       in0=x[:, tap:tap + S],
                                                       scalar=cols[:, w + tap:w + tap + 1],
                                                       in1=(ping, pong)[(tap + 1) % 2], op0=ALU.mult, op1=ALU.add))
                        own.settle()
                    V.tensor_scalar(pong, pong, cols[:, COL_CONVB + c:COL_CONVB + c + 1], None, ALU.add
                                    ).then_inc(sem("conv_done"), 1)
                if c >= 1:
                    d = c - 1
                    dve.wait_ge(sem("qkv_made"), d + 1)
                    if d >= 2:
                        dve.wait_ge(sem("scored"), d - 1)
                    V.tensor_copy(M.qk[:, d % 2], bank[2 + d % 2][:, :].rearrange("p (a s) -> p a s", a=2)
                                  ).then_inc(sem("qk_ready"), 1)
                if c >= 2 and (c - 2) % CPH == CPH - 1 or c == IC:
                    h = (c - 2) // CPH if c < IC else M_HEADS - 1
                    dve.wait_ge(sem("scored"), (h + 1) * CPH)
                    V.tensor_scalar(M.p[:, h], bank[6][:, 0:384], HD ** -0.5, None, ALU.mult
                                    ).then_inc(sem("s_taken"), 1)
            own.did(V.tensor_tensor(M.pre, bank[7][:, 0:16].rearrange("p (t n) -> p t n", t=TC),
                                    gate_b[:, :].unsqueeze(1).broadcast_to([P, TC, 2 * M_HEADS]), ALU.add))
            own.settle()
            V.tensor_scalar(M.lf, M.pre[:, :, M_HEADS:], 0.0, None, ALU.min).then_inc(sem("pre_ready"), 1)
            dve.wait_ge(sem("log_ready"), 1)
            V.tensor_tensor(M.lf, M.lf, M.fa, ALU.subtract).then_inc(sem("lf_ready"), 1)
            dve.wait_ge(sem("b_made"), 1)
            b_psum = bank[2][:, 0:TC * M_HEADS].rearrange("p (t n) -> p t n", t=TC)
            own.did(V.tensor_copy(M.b, b_psum))
            V.tensor_tensor(M.aa, M.pre[:, :, 0:M_HEADS], b_psum, ALU.subtract).then_inc(sem("a_ready"), 1)
            own.did(V.memset(M.mrow[0:M_HEADS, :, 0:P], 0.0))
            dve.wait_ge(sem("a_turned"), 1)
            own.did(V.tensor_scalar(M.mrow[0:M_HEADS, 0, P:], bank[3][0:M_HEADS, 0:S], 0.0, None, ALU.max))
            own.settle()
            shift, cur, doublings = 1, 0, 0
            while shift < S:
                V.tensor_tensor(M.mrow[0:M_HEADS, 1 - cur, P:], M.mrow[0:M_HEADS, cur, P:],
                                M.mrow[0:M_HEADS, cur, P - shift:P + S - shift], ALU.max
                                ).then_inc(sem("max_row"), 1)
                shift, cur, doublings = shift * 2, 1 - cur, doublings + 1
                dve.wait_ge(sem("max_row"), doublings)
            assert cur == 0 and doublings == DOUBLINGS
            dve.wait_ge(sem("max_spread"), 1)
            V.tensor_tensor(M.mt, M.b, bank[2][:, 0:TC * M_HEADS].rearrange("p (t n) -> p t n", t=TC), ALU.add
                            ).then_inc(sem("m_ready"), 1)
            for h in range(M_HEADS):
                far = bank[4 + h // 2][:, (h % 2) * S:(h % 2) * S + S]
                if h:
                    dve.wait_ge(sem("decay_ready"), h)
                own.did(V.tensor_scalar(M.ar[:, 0:S], far, M.aa[:, 0, h:h + 1], 0.0, ALU.subtract, ALU.max))
                V.tensor_scalar(M.ar[:, S:S + P], far[:, P:S], M.aa[:, 1, h:h + 1], 0.0, ALU.subtract, ALU.max
                                ).then_inc(sem("reach_ready"), 1)
                dve.wait_ge(sem("decay_ready"), h + 1)
                own.did(V.tensor_tensor(M.p[:, h], M.p[:, h], M.er, ALU.mult))
                own.settle()
                own.did(V.tensor_tensor(M.p[:, h, 0:P], M.p[:, h, 0:P], upto[:, :], ALU.mult))
                V.tensor_tensor(M.p[:, h, S:S + P], M.p[:, h, S:S + P], upto[:, :], ALU.mult
                                ).then_inc(sem("w_ready"), 1)
            dve.wait_ge(sem("em_ready"), 1)
            for h in range(M_HEADS):
                dve.wait_ge(sem("num_made"), h + 1)
                own.did(V.tensor_scalar(M.dm, bank[4][:, 2 * h:2 * h + 2], -1.0, None, ALU.mult))
                own.did(V.tensor_tensor(M.dn, bank[4][:, 2 * h:2 * h + 2], M.em[:, :, h], ALU.max))
                for t in range(TC):
                    own.did(V.bn_stats(M.st[:, t], bank[2 + t][:, :]))
                own.settle()
                own.did(V.tensor_tensor(M.dn, M.dn, M.dm, ALU.max))
                for t in range(TC):
                    own.did(V.bn_aggr(M.mv[:, t], M.st[:, t]))
                own.settle()
                own.did(V.reciprocal(M.rd, M.dn))
                own.settle()
                own.did(V.tensor_tensor(M.w2, M.mv[:, :, 1], M.rd, ALU.mult))
                own.settle()
                V.tensor_tensor(M.w2, M.w2, M.rd, ALU.mult).then_inc(sem("h_var"), 1)
                dve.wait_ge(sem("h_root"), h + 1)
                own.did(V.reciprocal(M.w1, M.w1))
                own.settle()
                own.did(V.tensor_tensor(M.w1, M.w1, M.rd, ALU.mult))
                own.settle()
                if h >= 2:
                    dve.wait_ge(sem("hn_turned"), 2 * (h - 1))
                for t in range(TC):
                    V.tensor_scalar(M.hn[:, t, (h % 2) * HD:(h % 2) * HD + HD], bank[2 + t][:, :], M.mv[:, t, 0:1],
                                    M.w1[:, t:t + 1], ALU.subtract, ALU.mult).then_inc(sem("hn_ready"), 1)
                for j in range(2):
                    dve.wait_ge(sem("hn_turned"), 2 * h + j + 1)
                    for cc in range(2):
                        c = h * CPH + 2 * j + cc
                        V.scalar_tensor_tensor(
                            out=M.sxc[:, c], in0=bank[5][:, cc * S:(cc + 1) * S],
                            scalar=cols[:, COL_GOUT + c:COL_GOUT + c + 1],
                            in1=M.sxc[:, c], op0=ALU.mult, op1=ALU.add).then_inc(sem("hT_taken"), 1)
            for t in range(TC):
                layer_norm(2, t, lambda t, half: dve.wait_ge(sem("y_ready"), 4 + 2 * t + half + 1))
            moe(1)

        @block.tensor
        def _(pe):
            mm = nc.tensor.matmul

            for half in range(2):
                pe.wait_ge(sem(f"xT_in{half}"), 16)
                pe.wait_ge(sem(f"w_in{half}"), 16)
                for k in range(half * DC // 2, (half + 1) * DC // 2):
                    for t in range(TC):
                        xk = xT[:, k, t * P:(t + 1) * P]
                        mm(bank[t][:, :], xk, win[:, k, 0:512], start=(k == 0), stop=(k == DC - 1))
                        last = mm(bank[2 + t][:, 0:ROPE], xk, win[:, k, 512:576], start=(k == 0), stop=(k == DC - 1))
            last.then_inc(sem("c_ready"), 1)
            pe.wait_ge(sem("consts"), 1)
            pe.wait_ge(sem("cn_ready"), 2 * TC)
            for t in range(TC):
                ts = slice(t * P, (t + 1) * P)
                for k in range(RC):
                    nc.tensor.transpose(bank[4][:, k * S + t * P:k * S + t * P + P], A.cn[:, t, k * P:(k + 1) * P],
                                        ident[:, :])
                    nc.tensor.transpose(bank[5][:, k * S + t * P:k * S + t * P + P],
                                        A.cn[:, t, 256 + k * P:256 + (k + 1) * P], ident[:, :])
                    last = nc.tensor.transpose(bank[6][:, k * S + t * P:k * S + t * P + P],
                                               A.kr[:, t, k].rearrange("p r f -> p (r f)"), ident[:, :])
            last.then_inc(sem("cT_ready"), 1)

            pe.wait_ge(sem("w_uq_in"), 16)
            pe.wait_ge(sem("w_ukv_in"), 16)
            pe.wait_ge(sem("cqT_ready"), 2)
            for i, (what, j) in enumerate(PROJ):
                if i >= 4:
                    pe.wait_ge(sem("proj_by_act" if i % 2 == 0 else "proj_by_dve"), (i - 4) // 2 + 1)
                if (what, j) == ("kn", 0):
                    pe.wait_ge(sem("ckvT_ready"), 2)
                out_bank = bank[i % 4]
                if what == "v":
                    t, n = divmod(j, 2)
                    for k in range(RC):
                        last = mm(out_bank[:, :], A.ckvT[:, k, t * P:(t + 1) * P],
                                  wukv[:, k, 1024 + n * 512:1024 + n * 512 + 512], start=(k == 0), stop=(k == RC - 1))
                else:
                    w, base, rhs = {"qn": (wuq, 0, A.cqT), "qpe": (wuq, 1024, A.cqT), "kn": (wukv, 0, A.ckvT)}[what]
                    for b in range(2):
                        col = base + (2 * j + b) * P
                        for k in range(RC):
                            last = mm(out_bank[:, b * S:(b + 1) * S], w[:, k, col:col + P], rhs[:, k],
                                      start=(k == 0), stop=(k == RC - 1))
                last.then_inc(sem("proj_made"), 1)

            pe.wait_ge(sem("rotated"), HEADS // HEADS_PER_ROPE)
            pe.wait_ge(sem("kpe_of_ready"), HEADS_PER_ROPE)
            pe.wait_ge(sem("proj_by_act"), len(PROJ) // 2)
            pe.wait_ge(sem("proj_by_dve"), len(PROJ) // 2)
            for i in range(HEADS + 2):
                if i < HEADS:
                    grp, j = divmod(i, HEADS_PER_ROPE)
                    if i >= 2:
                        pe.wait_ge(sem("exp_ready"), 2 * (i - 1))
                    for q, (lo, n) in enumerate(((0, P), (P, S))):
                        dst, qs = bank[i % 2][:, lo:lo + n], slice(q * P, (q + 1) * P)
                        mm(dst, A.qn[:, i, qs], A.kn[:, i, 0:n], start=True, stop=False, skip_group_check=True)
                        for b in range(2):
                            mm(dst, A.qpe[:, grp, b, qs], A.kpe_of[:, j, b, 0:n], start=False, stop=False,
                               skip_group_check=True)
                        last = mm(bank[i % 2][:, lo + n - P:lo + n], ident_bf[:, :], causal_bf[:, :], start=False,
                                  stop=True, skip_group_check=True)
                    last.then_inc(sem("s_made"), 1)
                if 1 <= i <= HEADS:
                    h = i - 1
                    pe.wait_ge(sem("p_ready"), 2 * i)
                    if h >= 2:
                        pe.wait_ge(sem("pT_ready"), h - 1)
                    for b, col in enumerate((0, P, S)):
                        last = nc.tensor.transpose(bank[2 + h % 2][:, col:col + P], A.p[:, h % 2, col:col + P],
                                                   ident[:, :])
                    last.then_inc(sem("p_turned"), 1)
                if i >= 2:
                    h = i - 2
                    pe.wait_ge(sem("pT_ready"), h + 1)
                    if h >= 2:
                        pe.wait_ge(sem("oT_ready"), h - 1)
                    vs = slice(h * P, (h + 1) * P)
                    mm(bank[4 + h % 2][:, 0:S], A.val[:, 0, vs], A.pT[:, h % 2, 0:S], start=True, stop=False,
                       skip_group_check=True)
                    mm(bank[4 + h % 2][:, P:S], A.val[:, 1, vs], A.pT[:, h % 2, S:384], start=False, stop=True,
                       skip_group_check=True).then_inc(sem("o_made"), 1)

            pe.wait_ge(sem("w_o_in"), 16)
            pe.wait_ge(sem("oT_ready"), HEADS)
            for t in range(TC):
                for half in range(2):
                    for h in range(HEADS):
                        last = mm(bank[LN.mla[t][half]][:, :], A.oT[:, h, t * P:(t + 1) * P],
                                  wo[:, h, half * 512:half * 512 + 512], start=(h == 0), stop=(h == HEADS - 1))
                    last.then_inc(sem("y_ready"), 1)

            def turn_x(n):
                for t in range(TC):
                    pe.wait_ge(sem("ln_done"), n * TC + t + 1)
                    for k in range(DC):
                        last = nc.tensor.transpose(bank[TURN_BANKS[t] + k // 4][:, (k % 4) * P:(k % 4) * P + P],
                                                   x_tok[:, t, k * P:(k + 1) * P], ident[:, :])
                    last.then_inc(sem("xT_made"), 1)

            def moe(layer):
                s = f"moe{layer}_"
                turn_x(2 * layer)
                if layer == 0:
                    pe.wait_ge(sem("small_in"), 16 * 5)
                pe.wait_ge(sem("xT_ready"), (4, 12)[layer])
                for t in range(TC):
                    for k in range(DC):
                        last = mm(bank[6][:, t * EXPERTS:(t + 1) * EXPERTS], xT[:, k, t * P:(t + 1) * P],
                                  router_w[:, k, :], start=(k == 0), stop=(k == DC - 1))
                last.then_inc(sem("logits"), 1)
                for b in range(4):
                    mm(bank[b][:, :], zeros_bf[:, 0:P], zeros_bf[:, :], start=True, stop=False, skip_group_check=True)
                pe.wait_ge(sem("mask_ready"), layer + 1)
                mm(bank[7][:, 0:16], before[:, :], E.mask[:, 0], start=True, stop=True)
                mm(bank[7][:, 16:32], before[:, :], E.mask[:, 1], start=True, stop=False)
                mm(bank[7][:, 16:32], ones[:, :], E.mask[:, 0], start=False, stop=True)
                mm(bank[7][:, 64:80], ones[:, :], E.mask[:, 0], start=True, stop=False)
                mm(bank[7][:, 64:80], ones[:, :], E.mask[:, 1], start=False, stop=True).then_inc(sem("places"), 1)
                pe.wait_ge(sem(f"moe{layer}_rounds"), 1)
                extra = extra_pairs(pe, layer)

                def gather():
                    for k in range(DC):
                        for i in range(3 * TC):
                            part, t = divmod(i, TC)
                            last = mm(bank[6 + k // 4][:, (k % 4) * P:(k % 4) * P + P],
                                      E.parts[:, part, t, k * P:(k + 1) * P],
                                      E.oh[:, t].rearrange("p a s -> p (a s)"), start=(i == 0), stop=(i == 3 * TC - 1))
                    last.then_inc(sem(s + "gathered"), 1)

                pe.wait_ge(sem("x_part2"), (layer + 1) * TC)
                pe.wait_ge(sem(s + "oh"), 1)
                gather()
                side = (slice(0, SLOTS), slice(SLOTS, 2 * SLOTS))
                with pe.Fori(0, extra + PAIRS) as g:
                    pe.wait_ge(sem(s + "ohg"), g + 1)
                    pe.wait_ge(sem(s + "xg_by_dve"), g + 1)
                    for t in range(TC):
                        last = nc.tensor.transpose(bank[6][:, t * P:(t + 1) * P],
                                                   E.ohg[:, t].rearrange("p a s -> p (a s)"), ident[:, :])
                    last.then_inc(sem(s + "gates_turned"), 1)
                    pe.wait_ge(sem(s + "xg_by_act"), g + 1)
                    for k in range(DC):
                        pe.wait_ge(sem(LANDED[layer].format(k)), g * 16 + 16 + LANDED_BEFORE[layer])
                        w = slot(k).rearrange("p (m a f) -> p m a f", m=2, a=2)
                        for m in range(2):
                            for e in range(2):
                                last = mm(bank[4 + m][side[e], :], E.xg[:, k, side[e]], w[:, m, e],
                                          start=(k == 0), stop=(k == DC - 1), skip_group_check=True)
                        last.then_inc(sem(s + "used"), 1)
                    pe.wait_ge(sem(s + "oh"), g + 2)
                    pe.wait_ge(sem(s + "gates"), g + 1)
                    gather()
                    pe.wait_ge(sem(s + "h"), g + 1)
                    for f in range(FC):
                        last = nc.tensor.transpose(bank[4][:, f * P:(f + 1) * P], E.h[:, f * P:(f + 1) * P],
                                                   ident[:, :])
                    last.then_inc(sem(s + "h_turned"), 1)
                    pe.wait_ge(sem(s + "hT"), g + 1)
                    for half in range(2):
                        for j in range(2):
                            u = DC + 2 * half + j
                            pe.wait_ge(sem(LANDED[layer].format(u)), g * 16 + 16 + LANDED_BEFORE[layer])
                            w = slot(u).rearrange("p (f a n) -> p f a n", f=2, a=2)
                            for ff in range(2):
                                for e in range(2):
                                    f = 2 * j + ff
                                    last = mm(bank[5 - half][side[e], :], E.hT[:, f, side[e]], w[:, ff, e],
                                              start=(f == 0), stop=(f == FC - 1), skip_group_check=True)
                            last.then_inc(sem(s + "used"), 1)
                    for half in range(2):
                        pe.wait_ge(sem(s + f"ye{half}"), g + 1)
                        for t in range(TC):
                            mm(bank[LN.moe[t][half]][:, :], E.gt_sb[:, t], E.ye[:, half], start=False, stop=False,
                               skip_group_check=True).then_inc(sem(s + "added"), 1)

            moe(0)

            turn_x(1)
            pe.wait_ge(sem("xT_ready"), 2 * 2 * TC)

            def unit_landed(u):
                pe.wait_ge(sem(LANDED[1].format(u % RING)), 16 * (u // RING + 1))

            def inner(c, out_bank, name):
                if c % 2 == 0:
                    unit_landed(c // 2)
                w = slot(c // 2 % RING).rearrange("p (c k n) -> p c k n", c=2, k=DC)
                for k in range(DC):
                    last = mm(out_bank[:, 0:S], w[:, c % 2, k], xT[:, k], start=(k == 0), stop=(k == DC - 1))
                last.then_inc(sem(name), 1)

            for i in range(IC + 2):
                if i < IC:
                    if i >= 2:
                        pe.wait_ge(sem("xm_ready"), i - 1)
                    inner(i, bank[i % 2], "xm_made")
                if 1 <= i <= IC:
                    c = i - 1
                    pe.wait_ge(sem("w3_made"), c + 1)
                    pe.wait_ge(sem("xc_ready"), c + 1)
                    if c >= 2:
                        pe.wait_ge(sem("qk_ready"), c - 1)
                        pe.wait_ge(sem("v_ready"), 2 * (c - 1))
                    w3, xc, xm = M.w3[:, c % 2], M.xc[:, c % 2], M.xm[:, c % 4, TAPS - 1:]
                    mm(bank[2 + c % 2][:, 0:S], w3[:, 0], xc, start=True, stop=True)
                    mm(bank[2 + c % 2][:, S:], w3[:, 1], xc, start=True, stop=True)
                    for t in range(TC):
                        mm(bank[4 + c % 2][:, t * P:(t + 1) * P], xm[:, t * P:(t + 1) * P], w3[:, 2],
                           start=True, stop=True)
                    mm(bank[4 + c % 2][:, S:], w3[:, 2], xm, start=True, stop=True).then_inc(sem("qkv_made"), 1)
                if i >= 2:
                    c = i - 2
                    pe.wait_ge(sem("qk_ready"), c + 1)
                    pe.wait_ge(sem("v_ready"), 2 * (c + 1))
                    q, k, v = M.qk[:, c % 2, 0], M.qk[:, c % 2, 1], M.vT[:, c % 2]
                    h, first = divmod(c, CPH)
                    if h and first == 0:
                        pe.wait_ge(sem("s_taken"), h)
                    mm(bank[6][:, 0:S], k[:, 0:P], q, start=(first == 0), stop=False, skip_group_check=True)
                    mm(bank[6][:, S:S + P], k[:, P:S], q[:, P:S], start=False, stop=False, skip_group_check=True)
                    for part, src in enumerate((q, k, v)):
                        for t in range(TC):
                            last = mm(bank[7][:, t * 8:t * 8 + 8], src[:, t * P:(t + 1) * P],
                                      gate_w[:, part * IC + c], start=(c == part == t == 0), stop=False,
                                      skip_group_check=True)
                    last.then_inc(sem("scored"), 1)

            def z(c):
                if c < 2:
                    pe.wait_ge(sem("xm_ready"), IC)
                else:
                    pe.wait_ge(sem("z_ready"), c - 1)
                inner(IC + c, bank[c % 2], "z_made")

            for c in range(4):
                z(c)
            pe.wait_ge(sem("lf_ready"), 1)
            mm(bank[2][:, 0:4], upto[:, :], M.lf[:, 0], start=True, stop=True)
            mm(bank[2][:, 4:8], upto[:, :], M.lf[:, 1], start=True, stop=False)
            mm(bank[2][:, 4:8], ones[:, :], M.lf[:, 0], start=False, stop=True).then_inc(sem("b_made"), 1)
            z(4)
            pe.wait_ge(sem("a_ready"), 1)
            for t in range(TC):
                last = mm(bank[3][0:M_HEADS, t * P:(t + 1) * P], M.aa[:, t], ident[:, :], start=True, stop=True)
            last.then_inc(sem("a_turned"), 1)
            for c in range(5, 8):
                z(c)
            pe.wait_ge(sem("max_row"), DOUBLINGS)
            row = M.mrow[0:M_HEADS, 0, P:]
            for h in range(M_HEADS):
                mm(bank[4 + h // 2][:, (h % 2) * S:(h % 2) * S + S], head_row[:, h, :], row, start=True, stop=True)
            for t in range(TC):
                last = mm(bank[2][:, t * 4:t * 4 + 4], row[:, t * P:(t + 1) * P], ident[0:M_HEADS, 0:M_HEADS],
                          start=True, stop=True)
            last.then_inc(sem("max_spread"), 1)
            for c in range(8, IC):
                z(c)

            def head(h):
                pe.wait_ge(sem("w_ready"), M_HEADS if h == 0 else h + 1)
                if h:
                    pe.wait_ge(sem("hn_ready"), TC * h)
                else:
                    pe.wait_ge(sem("em_ready"), 1)
                vs = slice(h * HD, (h + 1) * HD)
                w = M.p[:, h]
                products = ((0, w[:, 0:P], 0, True, True), (1, w[:, P:S], 0, True, False),
                            (1, w[:, S:S + P], 1, False, True))
                for t, lhs, key, start, stop in products:
                    mm(bank[4][:, 2 * h + t:2 * h + t + 1], lhs, ones[:, 0:1], start=start, stop=stop)
                for t, lhs, key, start, stop in products:
                    last = mm(bank[2 + t][:, :], lhs, M.val[:, key, vs], start=start, stop=stop)
                last.then_inc(sem("num_made"), 1)

            def turn(h):
                pe.wait_ge(sem("hn_ready"), TC * (h + 1))
                for j in range(2):
                    if h or j:
                        pe.wait_ge(sem("hT_taken"), 2 * (2 * h + j))
                    for cc in range(2):
                        ch = (h % 2) * HD + (2 * j + cc) * P
                        for t in range(TC):
                            last = nc.tensor.transpose(bank[5][:, cc * S + t * P:cc * S + t * P + P],
                                                       M.hn[:, t, ch:ch + P], ident[:, :])
                    last.then_inc(sem("hn_turned"), 1)

            def way_out(h):
                pe.wait_ge(sem("u_ready"), h + 1)
                if h == 0:
                    pe.wait_ge(sem("z_ready"), IC)
                    pe.wait_ge(sem("s_taken"), M_HEADS)
                for j in range(CPH // 2):
                    unit_landed(IC + h * CPH // 2 + j)
                for t in range(TC):
                    for half in range(2):
                        for c in range(h * CPH, (h + 1) * CPH):
                            u = IC + c // 2
                            w = slot(u % RING).rearrange("p (c n) -> p c n", c=2)
                            last = mm(bank[LN.mlstm[t][half]][:, :], M.zT[:, c, t * P:(t + 1) * P],
                                      w[:, c % 2, half * 512:half * 512 + 512], start=(c == 0), stop=(c == IC - 1),
                                      skip_group_check=True)
                            if (t, half) == (TC - 1, 1) and c % 2 and c < IC - 1:
                                last.then_inc(sem("out_used"), 1)
                        if h == M_HEADS - 1:
                            last.then_inc(sem("y_ready"), 1)

            head(0)
            for h in range(M_HEADS):
                turn(h)
                if h + 1 < M_HEADS:
                    head(h + 1)
                if h:
                    way_out(h - 1)
            way_out(M_HEADS - 1)
            moe(1)


def build(nc, shapes):
    a = {name: nc.dram_tensor(f"in_{name}", shape, dt, kind="ExternalInput").ap()
         for name, (shape, dt) in shapes.items()}
    out = nc.dram_tensor("out", (S, D), F32, kind="ExternalOutput").ap()
    build_trunk(nc, a, out)


def kernel(**inputs):
    import numpy as np
    from concourse import bacc
    from concourse.bass_utils import run_bass_kernel_spmd

    def get(name):
        return np.asarray(inputs[name])

    def columns(v):
        return v.reshape(-1, P).T

    arrays = {}
    x = get("x")[0]
    arrays["x"] = x
    arrays["xT"] = x.T.reshape(DC, P, S).transpose(1, 0, 2)
    arrays["positions"] = get("positions").reshape(S)
    arrays["mla_in"] = get("mla_w_in")[0].reshape(DC, P, 576).transpose(1, 0, 2)
    uq = get("mla_w_uq")[0].reshape(RC, P, HEADS, P + ROPE)
    rope = uq[..., P:].reshape(RC, P, HEADS // HEADS_PER_ROPE, HEADS_PER_ROPE, 2, HALF).transpose(0, 1, 2, 4, 3, 5)
    arrays["mla_uq"] = np.concatenate([uq[..., :P].reshape(RC, P, -1), rope.reshape(RC, P, -1)], -1).transpose(1, 0, 2)
    ukv = get("mla_w_ukv")[0].reshape(RC, P, HEADS, 2, P).transpose(1, 0, 3, 2, 4)
    arrays["mla_ukv"] = ukv.reshape(P, RC, 2048)
    arrays["mla_o"] = get("mla_w_o")[0].reshape(HEADS, P, D).transpose(1, 0, 2)
    inv_freq = np.float32(1) / np.float32(10000) ** (np.arange(0, ROPE, 2, dtype=np.float32) / np.float32(ROPE))
    arrays["cols"] = np.concatenate([
        columns(get("mla_g_q")[0]), columns(get("mla_g_kv")[0]),
        get("mlstm_conv_w")[0].reshape(TAPS, IC, P).transpose(2, 1, 0).reshape(P, -1),
        columns(get("mlstm_conv_b")[0]), columns(get("mlstm_g_out")[0]), columns(get("mlstm_skip")[0]),
        np.tile(inv_freq, P // HALF)[:, None]], 1)
    arrays["ln"] = np.stack([get("ln_g"), get("ln_b")], 2).reshape(4, 2, D)
    arrays["router_w"] = get("router_w").reshape(DC, P, EXPERTS).transpose(1, 0, 2)
    arrays["router_b"] = get("router_b")
    arrays["gate_b"] = np.concatenate([get("mlstm_b_ig")[0], get("mlstm_b_fg")[0]])
    arrays["gate_w"] = np.concatenate([get("mlstm_w_ig")[0], get("mlstm_w_fg")[0]], -1
                                      ).reshape(3 * IC, P, 2 * M_HEADS).transpose(1, 0, 2)
    arrays["w_blocks"] = np.stack([get(f"mlstm_w_{n}")[0].reshape(IC, P, BLK).transpose(1, 0, 2) for n in "qkv"], 1)
    up = np.stack([get("moe_w_gate"), get("moe_w_up")]).reshape(2, 2, PAIRS, 2, DC, P, FF)
    up = up.transpose(1, 2, 4, 5, 0, 3, 6).reshape(2, PAIRS, DC, P, UNIT)
    down = get("moe_w_down").reshape(2, PAIRS, 2, 2, 2, P, 2, 512)
    down = down.transpose(0, 1, 6, 3, 5, 4, 2, 7).reshape(2, PAIRS, 4, P, UNIT)
    arrays["moe"] = np.concatenate([up, down], 2)
    m_in = get("mlstm_w_in")[0].reshape(DC, P, IC, 2, P).transpose(2, 1, 3, 0, 4).reshape(IC, P, UNIT)
    m_out = get("mlstm_w_out")[0].reshape(IC // 2, 2, P, D).transpose(0, 2, 1, 3).reshape(IC // 2, P, UNIT)
    arrays["mlstm"] = np.concatenate([m_in, m_out], 0)
    arrays = {n: np.ascontiguousarray(v) for n, v in arrays.items()}

    nc = bacc.Bacc("TRN2", target_bir_lowering=False, num_devices=1)
    build(nc, {n: (v.shape, mybir.dt.from_np(v.dtype)) for n, v in arrays.items()})
    result = run_bass_kernel_spmd(nc, [{f"in_{n}": v for n, v in arrays.items()}], core_ids=[0])
    return result.results[0]["out"].reshape(1, S, D)
```

```python
from contextlib import ExitStack

import concourse.bass as bass
from concourse import mybir

F32 = mybir.dt.float32
BF16 = mybir.dt.bfloat16
I32 = mybir.dt.int32
ALU = mybir.AluOpType
ACT = mybir.ActivationFunctionType
AX = mybir.AxisListType

P = 128
D = 1024
S = 256
TC = S // P
DC = D // P
HEADS = 8
Q_RANK = KV_RANK = 256
RC = Q_RANK // P
ROPE = 64
HALF = ROPE // 2
HEADS_PER_ROPE = P // HALF
SCALE = (128 + ROPE) ** -0.5
INNER = 2048
IC = INNER // P
M_HEADS = 4
CPH = IC // M_HEADS
HD = INNER // M_HEADS
TAPS = 4
BLK = 4
EXPERTS = 16
GROUPS = 4
PER_GROUP = 4
FF = 512
FC = FF // P
PAIRS = EXPERTS // 2
SLOTS = 64
MAX_ROUNDS = S // SLOTS
ALPHA = (2.0 * 2) ** 0.25
EPS = 1e-5
DOUBLINGS = S.bit_length() - 1
FAR = 1024.0
NEG = -1e30

RING = 12
UNIT = 2048
W_IN = 0
W_UQ = W_IN + DC * 576
W_UKV = W_UQ + RC * 1536
W_O = W_UKV + RC * 2048
M_UNITS_IN = IC
M_UNITS = IC + IC // 2

TWO_PI = 6.283185307179586
PI_A = 6.28125
PI_B = 0.0019350051879882812
PI_C = TWO_PI - PI_A - PI_B
V_COLS = P + 2 * M_HEADS
MAGIC = 1.5 * 2 ** 23

COL_GQ, COL_GKV, COL_CONVW, COL_CONVB = 0, 2, 4, 4 + TAPS * IC
COL_GOUT = COL_CONVB + IC
COL_SKIP = COL_GOUT + IC
COL_INVF = COL_SKIP + IC
COLS = COL_INVF + 1

class Steps:

    def __init__(self, engine, sem):
        self.engine, self.sem, self.n = engine, sem, 0

    def did(self, instruction):
        self.n += 1
        return instruction.then_inc(self.sem, 1)

    def settle(self):
        self.engine.wait_ge(self.sem, self.n)

def build_trunk(nc, a, out):
    with ExitStack() as ctx:
        sems = {}

        def sem(name):
            if name not in sems:
                sems[name] = ctx.enter_context(nc.semaphore(name))
            return sems[name]

        def sb(name, shape, dt=F32):
            return ctx.enter_context(nc.sbuf_tensor(name, shape, dt))

        bank = [ctx.enter_context(nc.psum_tensor(f"bank{i}", [P, 512], F32)) for i in range(8)]

        ring = sb("ring", [P, RING * UNIT])
        x_tok = sb("x_tok", [P, TC, D])
        xT = sb("xT", [P, DC, S])
        ln_gb = sb("ln_gb", [P, 2, D])
        cols = sb("cols", [P, COLS])
        ident = sb("ident", [P, P])
        ident_bf = sb("ident_bf", [P, P], BF16)
        causal_bf = sb("causal_bf", [P, P], BF16)
        upto = sb("upto", [P, P])
        before = sb("before", [P, P])
        ones = sb("ones", [P, P])
        alpha_ident = sb("alpha_ident", [P, P])
        slot_no = sb("slot_no", [P, SLOTS])
        stats = sb("stats", [P, TC, 2, 6])
        mean_var = sb("mean_var", [P, TC, 2])
        rstd = sb("rstd", [P, TC])
        lower = sb("lower", [P, PER_GROUP, PER_GROUP])
        router_b = sb("router_b", [P, EXPERTS])
        router_w = sb("router_w", [P, DC, EXPERTS])
        gate_b = sb("gate_b", [P, 2 * M_HEADS])
        gate_qk = sb("gate_qk", [P, IC, 2 * M_HEADS])
        gate_v = sb("gate_v", [P, IC, 2 * M_HEADS])
        w_blocks = sb("w_blocks", [P, 3, IC, BLK])
        block_mask = sb("block_mask", [P, P // BLK])
        half_pi = sb("half_pi", [P, 1])
        eps = sb("eps", [P, 1])
        head_row = sb("head_row", [M_HEADS, M_HEADS, P])
        extra_pairs_at = sb("extra_pairs_at", [P, 4], I32)

        arena_floats = 20100
        arena = sb("arena", [P, arena_floats])

        class Carve:
            def __init__(self):
                self.at = 0

            def __call__(self, *shape, dt=F32):
                n = 1
                for s in shape:
                    n *= s
                words = n if dt is F32 else (n + 1) // 2
                v = arena[:, self.at:self.at + words]
                self.at += words
                assert self.at <= arena_floats, self.at
                if dt is not F32:
                    v = v.bitcast(dt)
                if len(shape) > 1:
                    names = "abcd"[:len(shape)]
                    v = v.rearrange(f"p ({' '.join(names)}) -> p {' '.join(names)}",
                                    **dict(zip(names, shape)))
                return v

        block = ctx.enter_context(nc.Block())

        class A:
            v = Carve()
            ang = v(S)
            turns = v(2, S)
            posf = v(S)
            cos = v(S)
            sin = v(S)
            sq = v(2, 256)
            ss = v(TC, 2)
            rs = v(TC, 2)
            cn = v(TC, 512)
            kr = v(TC, 2, HEADS_PER_ROPE, HALF)
            cqT = v(RC, S)
            ckvT = v(RC, S)
            kpe = v(2, S)
            kpe_of = v(HEADS_PER_ROPE, 2, S)
            rt = v(2, 2, S)
            qpe = v(2, 2, S)
            qn = v(HEADS, S)
            kn = v(HEADS, S)
            val = v(TC, D)
            mx = v(HEADS, 2)
            nm = v(HEADS, 2)
            sm = v(HEADS, 2)
            rc = v(HEADS, 2)
            p = v(2, 384)
            pT = v(2, 384)
            oT = v(HEADS, S)
            gate_w = ring[:, (RING - 1) * UNIT:(RING - 1) * UNIT + 3 * IC * BLK * 2 * M_HEADS].rearrange(
                "p (w c j n) -> p w c j n", w=3, c=IC, j=BLK)
            norm = qn.rearrange("p h s -> p (h s)").rearrange("p (t d) -> p t d", t=TC)

        class E:
            v = Carve()
            parts = v(3, TC, D, dt=BF16)
            rest = v(2, TC, D)
            norm = v(TC, D)
            lg = v(TC, EXPERTS)
            sc = v(TC, EXPERTS)
            sel = v(TC, EXPERTS)
            above = v(TC * GROUPS, PER_GROUP, PER_GROUP)
            tied = v(TC * GROUPS, PER_GROUP, PER_GROUP)
            rank = v(TC, EXPERTS)
            top = v(TC, EXPERTS)
            top_sel = v(TC, EXPERTS)
            gsum = v(TC, GROUPS)
            grank = v(TC, GROUPS)
            den = v(TC)
            rden = v(TC)
            gate = v(TC, EXPERTS)
            mask = v(TC, EXPERTS)
            posm = v(TC, EXPERTS)
            tot = v(EXPERTS)
            most = v(1)
            full_rounds = v(MAX_ROUNDS)
            over = v(MAX_ROUNDS)
            nrounds = v(1)
            posm_all = v(TC, MAX_ROUNDS * EXPERTS + 2)
            gate_all = v(TC, MAX_ROUNDS * EXPERTS + 2)
            oh = v(TC, 2, SLOTS, dt=BF16)
            ohg = v(TC, 2, SLOTS)
            gt_sb = v(TC, P)
            xg = v(DC, 2 * SLOTS)
            sg = v(FF)
            h = v(FF)
            hT = v(FC, 2 * SLOTS)
            ye = v(2, FF)

        class M:
            v = Carve()
            sxc = v(IC, S)
            zT = v(IC, S)
            val = v(TC, IC, V_COLS)
            p = v(M_HEADS, 384)
            gv = v(TC, 2 * M_HEADS)
            pre = v(TC, 2 * M_HEADS)
            fa = v(TC, M_HEADS)
            fb = v(TC, M_HEADS)
            lf = v(TC, M_HEADS)
            b = v(TC, M_HEADS)
            aa = v(TC, M_HEADS)
            mt = v(TC, M_HEADS)
            em = v(TC, M_HEADS)
            dn = v(2)
            dm = v(2)
            rd = v(2)
            st = v(TC, 6)
            mv = v(TC, 2)
            w1 = v(2)
            w2 = v(2)
            later = v.at
            xm = v(4, S + TAPS - 1)
            cv = v(2, S)
            cv2 = v(2, S)
            xc = v(3, S)
            w3 = v(2, 2 * P + V_COLS)
            qk = v(2, 2, S)
            v.at = later
            hn = v(TC, 2 * HD)
            norm = hn
            mrow = v(2, P + S)
            ar = v(384)
            er = v(384)

        class LN:
            mla = ((6, 7), (0, 1))
            moe = ((0, 1), (2, 3))
            mlstm = ((0, 1), (6, 7))

        LN_BANKS = (LN.mla, LN.moe, LN.mlstm, LN.moe)
        LN_STEPS = 2 * TC
        TURN_BANKS = (4, 2)
        LN_NORM = (A.norm, E.norm, M.norm, E.norm)

        win = ring[:, W_IN:W_UQ].rearrange("p (k n) -> p k n", k=DC)
        wuq = ring[:, W_UQ:W_UKV].rearrange("p (k n) -> p k n", k=RC)
        wukv = ring[:, W_UKV:W_O].rearrange("p (k n) -> p k n", k=RC)
        wo = ring[:, W_O:W_O + HEADS * D].rearrange("p (k n) -> p k n", k=HEADS)

        LANDED = ("slot{}_landed", "slot{}_landed_again")
        LANDED_BEFORE = (0, 16 * M_UNITS // RING)

        def extra_pairs(engine, layer):
            return engine.value_load(extra_pairs_at[0:1, layer:layer + 1], min_val=0,
                                     max_val=PAIRS * (MAX_ROUNDS - 1))

        def slot(u):
            return ring[:, u * UNIT:(u + 1) * UNIT]

        PROJ = [("qn", 0), ("qpe", 0), ("qn", 1), ("qpe", 1), ("qn", 2), ("kn", 0), ("qn", 3), ("kn", 1),
                ("kn", 2), ("kn", 3), ("v", 0), ("v", 1), ("v", 2), ("v", 3)]

        @block.sync
        def _(sp):
            def load(dst, src, name):
                sp.dma_start(dst, src).then_inc(sem(name), 16)

            for part in range(4):
                ks = slice(part * DC // 4, (part + 1) * DC // 4)
                load(xT[:, ks, :], a["xT"][:, ks, :], f"x_w_in{part}")
                load(win[:, ks, :], a["mla_in"][:, ks, :], f"x_w_in{part}")
            load(cols[:, :], a["cols"], "cols_in")
            load(A.ang.bitcast(I32), a["positions"].partition_broadcast(P), "pos_in")
            load(wuq, a["mla_uq"], "w_uq_in")
            load(wukv, a["mla_ukv"], "w_ukv_in")
            load(wo, a["mla_o"], "w_o_in")
            load(x_tok[:, :, :], a["x"].rearrange("(c p) d -> p c d", p=P), "x_in")
            load(ln_gb[:, :, :], a["ln"][0].partition_broadcast(P), "ln_gb_in")
            for name, dst, src in (("small", router_w[:, :, :], a["router_w"]),
                                   ("small", router_b[:, :], a["router_b"].partition_broadcast(P)),
                                   ("small", gate_b[:, :], a["gate_b"].partition_broadcast(P)),
                                   ("small", A.gate_w, a["gate_w"]),
                                   ("small", w_blocks[:, :, :, :], a["w_blocks"])):
                load(dst, src, "small_in")

            def next_ln(n):
                sp.wait_ge(sem("ln_done"), LN_STEPS * n)
                load(ln_gb[:, :, :], a["ln"][n].partition_broadcast(P), "ln_gb_in")

            def moe(layer, first_free, order=range(RING)):
                for u in order:
                    first_free(u)
                    load(slot(u), a["moe"][layer, 0, u], LANDED[layer].format(u))
                next_ln(2 * layer + 1)
                sp.wait_ge(sem(f"moe{layer}_rounds"), 1)
                extra = extra_pairs(sp, layer)
                with sp.Fori(0, extra + (PAIRS - 1)) as before_it:
                    for u in range(RING):
                        sp.wait_ge(sem(f"moe{layer}_used"), before_it * RING + (u + 1))
                        sp.dma_start(slot(u), a["moe"][layer, bass.ds((before_it + 1) % PAIRS, 1), u].rearrange("a p n -> (a p) n")
                                     ).then_inc(sem(LANDED[layer].format(u)), 16)
                return extra

            def mla_region_free(u):
                begin, end = u * UNIT, (u + 1) * UNIT
                if begin < W_UQ:
                    sp.wait_ge(sem("c_ready"), TC)
                if end > W_UQ and begin < W_O:
                    sp.wait_ge(sem("proj_made"), len(PROJ))
                if end > W_O and begin < W_O + HEADS * D:
                    sp.wait_ge(sem("y_ready"), 4)
                if u == RING - 1:
                    sp.wait_ge(sem("gate_w_made"), 1)

            extra = moe(0, mla_region_free, [10, 11, *range(10)])

            def mlstm_unit_used(u):
                if u < IC // 2:
                    sp.wait_ge(sem("xm_made"), 2 * u + 2)
                elif u < IC:
                    sp.wait_ge(sem("z_made"), 2 * (u - IC // 2) + 2)
                elif u < M_UNITS - 1:
                    sp.wait_ge(sem("out_used"), u - IC + 1)
                else:
                    sp.wait_ge(sem("y_ready"), 8)

            for u in range(M_UNITS):
                if u < RING:
                    sp.wait_ge(sem("moe0_used"), extra * RING + (PAIRS - 1) * RING + u + 1)
                else:
                    mlstm_unit_used(u - RING)
                load(slot(u % RING), a["mlstm"][u], LANDED[1].format(u % RING))
                if u == RING - 1:
                    next_ln(2)

            moe(1, lambda u: mlstm_unit_used(M_UNITS - RING + u))
            for t in range(TC):
                sp.wait_ge(sem("ln_done"), 3 * LN_STEPS + 2 * t + 2)
                sp.dma_start(out.rearrange("(c p) d -> p c d", p=P)[:, t, :], x_tok[:, t, :]
                             ).then_inc(sem("stored"), 16)
            sp.wait_ge(sem("stored"), 16 * TC)

        @block.gpsimd
        def _(pool):
            own = Steps(pool, sem("pool_steps"))

            def select(dst, src, pattern, op, fill, base, mul):
                own.did(nc.gpsimd.affine_select(out=dst, in_=src, pattern=pattern, compare_op=op, fill=fill,
                                                base=base, channel_multiplier=mul))

            own.did(nc.gpsimd.memset(ident[:, :], 0.0))
            own.did(nc.gpsimd.memset(ones[:, :], 1.0))
            own.did(nc.gpsimd.memset(causal_bf[:, :], 0.0))
            own.did(nc.gpsimd.memset(alpha_ident[:, :], 0.0))
            own.did(nc.gpsimd.memset(eps[:, :], EPS))
            own.did(nc.gpsimd.memset(half_pi[:, :], TWO_PI / 4))
            own.did(nc.gpsimd.memset(block_mask[:, :], 1.0))
            own.did(nc.gpsimd.memset(lower[:, :, :], 1.0))
            own.did(nc.gpsimd.memset(head_row[:, :, :], 0.0))
            own.did(nc.gpsimd.memset(A.kpe_of, 0.0))
            own.did(nc.gpsimd.iota(slot_no[:, :], [[1, SLOTS]], base=0, channel_multiplier=0,
                                   allow_small_or_imprecise_dtypes=True))
            own.settle()
            select(ident[:, :], ident[:, :], [[-1, P]], ALU.not_equal, 1.0, 0, 1)
            select(alpha_ident[:, :], alpha_ident[:, :], [[-1, P]], ALU.not_equal, ALPHA, 0, 1)
            select(causal_bf[:, :], causal_bf[:, :], [[-1, P]], ALU.is_ge, NEG, 0, 1)
            select(upto[:, :], ones[:, :], [[1, P]], ALU.is_ge, 0.0, 0, -1)
            select(before[:, :], ones[:, :], [[1, P]], ALU.is_gt, 0.0, 0, -1)
            select(block_mask[:, :], block_mask[:, :], [[-BLK, P // BLK]], ALU.is_ge, 0.0, 0, 1)
            select(lower[:, :, :], lower[:, :, :], [[1, PER_GROUP], [-1, PER_GROUP]], ALU.is_gt, 0.0, 0, 0)
            select(head_row[:, :, :], head_row[:, :, :], [[-1, M_HEADS], [0, P]], ALU.not_equal, 1.0, 0, 1)
            own.settle()
            select(block_mask[:, :], block_mask[:, :], [[BLK, P // BLK]], ALU.is_gt, 0.0, BLK, -1)
            nc.gpsimd.tensor_copy(ident_bf[:, :], ident[:, :]).then_inc(sem("consts"), 1)

            pool.wait_ge(sem("kpe_ready"), 1)
            for j in range(HEADS_PER_ROPE):
                rows = slice(j * HALF, (j + 1) * HALF)
                nc.gpsimd.tensor_copy(A.kpe_of[rows, j], A.kpe[rows]).then_inc(sem("kpe_of_ready"), 1)

            pool.wait_ge(sem("small_in"), 16 * 5)
            pool.wait_ge(sem("kpe_of_ready"), HEADS_PER_ROPE)
            own.did(nc.gpsimd.tensor_tensor(A.gate_w, A.gate_w, w_blocks[:, :, :, :].unsqueeze(4).broadcast_to(
                [P, 3, IC, BLK, 2 * M_HEADS]), ALU.mult))
            own.settle()

            def add(dst, x, y):
                own.did(nc.gpsimd.tensor_tensor(dst, x, y, ALU.add))

            add(A.gate_w[:, :, :, 0], A.gate_w[:, :, :, 0], A.gate_w[:, :, :, 1])
            add(A.gate_w[:, :, :, 2], A.gate_w[:, :, :, 2], A.gate_w[:, :, :, 3])
            own.settle()
            add(A.gate_w[:, 0:2, :, 0], A.gate_w[:, 0:2, :, 0], A.gate_w[:, 0:2, :, 2])
            add(gate_v[:, :, :], A.gate_w[:, 2, :, 0], A.gate_w[:, 2, :, 2])
            own.settle()
            nc.gpsimd.tensor_tensor(gate_qk[:, :, :], A.gate_w[:, 0, :, 0], A.gate_w[:, 1, :, 0], ALU.add
                                    ).then_inc(sem("gate_w_made"), 1)

            def moe(layer):
                s = f"moe{layer}_"
                for t in range(TC):
                    pool.wait_ge(sem("x_part0"), layer * TC + t + 1)
                    nc.gpsimd.tensor_tensor(E.rest[:, 0, t], x_tok[:, t], E.parts[:, 0, t], ALU.subtract
                                            ).then_inc(sem("x_rest0"), 1)
                for t in range(TC):
                    pool.wait_ge(sem("x_part1"), layer * TC + t + 1)
                    nc.gpsimd.tensor_tensor(E.rest[:, 1, t], E.rest[:, 0, t], E.parts[:, 1, t], ALU.subtract
                                            ).then_inc(sem("x_rest1"), 1)

                def gates_of(g):
                    pool.wait_ge(sem(s + "oh"), g + 1)
                    nc.gpsimd.tensor_tensor(
                        E.ohg, E.oh, E.gate_all[:, :, bass.ds(g * 2, 2)].unsqueeze(3).broadcast_to([P, TC, 2, SLOTS]),
                        ALU.mult).then_inc(sem(s + "ohg"), 1)

                gates_of(0)
                pool.wait_ge(sem(f"moe{layer}_rounds"), 1)
                extra = extra_pairs(pool, layer)
                with pool.Fori(1, extra + PAIRS) as g:
                    pool.wait_ge(sem(s + "gates_turned"), g)
                    gates_of(g)

            moe(0)

            pool.wait_ge(sem("ln_done"), 2 * LN_STEPS)
            for c in range(IC):
                if c >= 2:
                    pool.wait_ge(sem("qkv_made"), c - 1)
                own.did(nc.gpsimd.tensor_copy(M.w3[:, c % 2, 3 * P:], gate_v[:, c]))
                made = nc.gpsimd.tensor_tensor(
                    M.w3[:, c % 2, 0:3 * P].rearrange("p (w g j) -> p w g j", w=3, j=BLK),
                    block_mask[:, :].unsqueeze(1).unsqueeze(3).broadcast_to([P, 3, P // BLK, BLK]),
                    w_blocks[:, :, c].unsqueeze(2).broadcast_to([P, 3, P // BLK, BLK]), ALU.mult)
                made.then_inc(sem("w3_made"), 1)
                own.settle()
            for i in range(IC // 2):
                cs = slice(2 * i, 2 * i + 2)
                pool.wait_ge(sem("hT_taken"), 2 * i + 2)
                pool.wait_ge(sem("z_ready"), 2 * i + 2)
                nc.gpsimd.tensor_tensor(M.zT[:, cs], M.sxc[:, cs], M.zT[:, cs], ALU.mult).then_inc(sem("u_ready"), 1)
            moe(1)

        @block.scalar
        def _(act):
            own = Steps(act, sem("act_steps"))

            def rstd_root(n, t):
                act.wait_ge(sem("ln_var"), n * TC + t + 1)
                nc.scalar.activation(rstd[:, t:t + 1], mean_var[:, t, 1:2], ACT.Sqrt, bias=eps[:, :]
                                     ).then_inc(sem("ln_root"), 1)

            def turned_x(n):
                for t in range(TC):
                    for j in range(2):
                        act.wait_ge(sem("xT_made"), LN_STEPS * n + 2 * t + j + 1)
                        nc.scalar.copy(xT[:, j * 4:j * 4 + 4, t * P:(t + 1) * P],
                                       bank[TURN_BANKS[t] + j][:, :].rearrange("p (k s) -> p k s", k=4)
                                       ).then_inc(sem("xT_ready"), 1)

            act.wait_ge(sem("consts"), 1)
            act.wait_ge(sem("ang_ready"), 1)
            own.did(nc.scalar.activation(A.sin, A.turns[:, 0], ACT.Sin))
            own.did(nc.scalar.activation(A.cos, A.turns[:, 0], ACT.Abs))
            own.settle()
            nc.scalar.activation(A.cos, A.cos, ACT.Sin, scale=-1.0, bias=half_pi[:, :]).then_inc(sem("rope_ready"), 1)
            for t in range(TC):
                act.wait_ge(sem("c_ready"), t + 1)
                for part in range(2):
                    own.did(nc.scalar.activation(A.sq[:, part], bank[t][:, part * 256:part * 256 + 256], ACT.Square,
                                                 accum_out=A.ss[:, t, part:part + 1]))
                own.settle()
                nc.scalar.activation(A.rs[:, t], A.ss[:, t], ACT.Sqrt, scale=1.0 / Q_RANK, bias=eps[:, :]
                                     ).then_inc(sem("c_root"), 1)
            act.wait_ge(sem("cT_ready"), 1)
            act.wait_ge(sem("cols_in"), 16)
            for k in range(RC):
                nc.scalar.activation(A.ckvT[:, k], bank[5][:, k * S:(k + 1) * S], ACT.Identity,
                                     scale=cols[:, COL_GKV + k:COL_GKV + k + 1]).then_inc(sem("ckvT_ready"), 1)

            def project_out(i, dst, src):
                act.wait_ge(sem("proj_made"), i + 1)
                nc.scalar.copy(dst, src).then_inc(sem("proj_by_act"), 1)

            for i, (what, j) in enumerate(PROJ):
                if i % 2 == 0:
                    if what == "v":
                        project_out(i, A.val[:, j // 2, (j % 2) * 512:(j % 2) * 512 + 512], bank[i % 4][:, :])
                    else:
                        project_out(i, (A.qn if what == "qn" else A.kn)[:, 2 * j:2 * j + 2],
                                    bank[i % 4][:, :].rearrange("p (a s) -> p a s", a=2))
            for i in range(HEADS + 1):
                if i < HEADS:
                    act.wait_ge(sem("max_ready"), i + 1)
                    if i >= 2:
                        act.wait_ge(sem("p_turned"), i - 1)
                    for b, (lo, hi) in enumerate(((0, 128), (128, 384))):
                        nc.scalar.activation(A.p[:, i % 2, lo:hi], bank[i % 2][:, lo:hi], ACT.Exp, scale=SCALE,
                                             bias=A.nm[:, i, b:b + 1], accum_out=A.sm[:, i, b:b + 1]
                                             ).then_inc(sem("exp_ready"), 1)
                if i >= 1:
                    act.wait_ge(sem("p_turned"), i)
                    if i >= 3:
                        act.wait_ge(sem("o_made"), i - 2)
                    nc.scalar.copy(A.pT[:, (i - 1) % 2], bank[2 + (i - 1) % 2][:, 0:384]).then_inc(sem("pT_ready"), 1)
            for t in range(TC):
                rstd_root(0, t)

            def moe(layer):
                s = f"moe{layer}_"
                ln = 2 * layer + 1
                turned_x(2 * layer)
                for t in range(TC):
                    act.wait_ge(sem("ln_done"), 2 * layer * LN_STEPS + 2 * t + 2)
                    nc.scalar.copy(E.parts[:, 0, t], x_tok[:, t]).then_inc(sem("x_part0"), 1)
                for t in range(TC):
                    act.wait_ge(sem("x_rest0"), layer * TC + t + 1)
                    nc.scalar.copy(E.parts[:, 1, t], E.rest[:, 0, t]).then_inc(sem("x_part1"), 1)
                act.wait_ge(sem("logits"), layer + 1)
                nc.scalar.activation(E.sc, bank[6][:, 0:TC * EXPERTS].rearrange("p (t e) -> p t e", t=TC), ACT.Sigmoid
                                     ).then_inc(sem("scores"), 1)
                for t in range(TC):
                    act.wait_ge(sem("x_rest1"), layer * TC + t + 1)
                    nc.scalar.copy(E.parts[:, 2, t], E.rest[:, 1, t]).then_inc(sem("x_part2"), 1)
                def gathered(count):
                    act.wait_ge(sem(s + "gathered"), count)
                    nc.scalar.copy(E.xg[:, 4:8], bank[7][:, :].rearrange("p (k s) -> p k s", k=4)
                                   ).then_inc(sem(s + "xg_by_act"), 1)

                gathered(1)
                act.wait_ge(sem(f"moe{layer}_rounds"), 1)
                extra = extra_pairs(act, layer)
                with act.Fori(0, extra + PAIRS) as g:
                    act.wait_ge(sem(s + "used"), g * RING + DC)
                    nc.scalar.activation(E.sg, bank[4][:, :], ACT.Silu).then_inc(sem(s + "silu"), 1)
                    gathered(g + 2)
                    act.wait_ge(sem(s + "h_turned"), g + 1)
                    nc.scalar.copy(E.hT, bank[4][:, :].rearrange("p (k s) -> p k s", k=FC)
                                   ).then_inc(sem(s + "hT"), 1)
                    act.wait_ge(sem(s + "used"), g * RING + RING)
                    nc.scalar.copy(E.ye[:, 1], bank[4][:, :]).then_inc(sem(s + "ye1"), 1)
                for t in range(TC):
                    rstd_root(ln, t)

            moe(0)

            turned_x(1)
            for c in range(IC + 2):
                if c < IC:
                    act.wait_ge(sem("xm_made"), c + 1)
                    if c >= 4:
                        act.wait_ge(sem("conv_done"), c - 3)
                        act.wait_ge(sem("qkv_made"), c - 3)
                    if c == 0:
                        act.wait_ge(sem("pads"), 1)
                    nc.scalar.copy(M.xm[:, c % 4, TAPS - 1:], bank[c % 2][:, 0:S]).then_inc(sem("xm_ready"), 1)
                    act.wait_ge(sem("conv_done"), c + 1)
                    if c >= 3:
                        act.wait_ge(sem("qkv_made"), c - 2)
                    nc.scalar.activation(M.xc[:, c % 3], M.cv[:, c % 2], ACT.Silu).then_inc(sem("xc_ready"), 1)
                    act.wait_ge(sem("xc_ready"), c + 1)
                    own.did(nc.scalar.activation(M.sxc[:, c], M.xc[:, c % 3], ACT.Copy,
                                                 scale=cols[:, COL_SKIP + c:COL_SKIP + c + 1]))
                if c >= 2:
                    d = c - 2
                    act.wait_ge(sem("qkv_made"), d + 1)
                    nc.scalar.copy(M.val[:, :, d],
                                   bank[4 + d % 2][:, 0:TC * V_COLS].rearrange("p (t n) -> p t n", t=TC)
                                   ).then_inc(sem("v_ready"), 1)
            def z_silu(c):
                act.wait_ge(sem("z_made"), c + 1)
                nc.scalar.activation(M.zT[:, c], bank[c % 2][:, 0:S], ACT.Silu).then_inc(sem("z_ready"), 1)
            z_silu(0)
            z_silu(1)
            act.wait_ge(sem("pre_ready"), 1)
            own.did(nc.scalar.activation(M.fa, M.pre[:, :, M_HEADS:], ACT.Abs))
            own.settle()
            own.did(nc.scalar.activation(M.fb, M.fa, ACT.Exp, scale=-1.0))
            own.settle()
            nc.scalar.activation(M.fa, M.fb, ACT.Ln, bias=1.0).then_inc(sem("log_ready"), 1)
            for c in range(2, 8):
                z_silu(c)
            act.wait_ge(sem("m_ready"), 1)
            nc.scalar.activation(M.em, M.mt, ACT.Exp, scale=-1.0).then_inc(sem("em_ready"), 1)
            for h in range(M_HEADS):
                act.wait_ge(sem("reach_ready"), h + 1)
                nc.scalar.activation(M.er, M.ar, ACT.Exp, scale=-1.0).then_inc(sem("decay_ready"), 1)
                z_silu(8 + h)
            for h in range(M_HEADS):
                act.wait_ge(sem("h_var"), h + 1)
                nc.scalar.activation(M.w1, M.w2, ACT.Sqrt, bias=eps[:, :]).then_inc(sem("h_root"), 1)
                if h < 2:
                    z_silu(12 + 2 * h)
                    z_silu(13 + 2 * h)
            for t in range(TC):
                rstd_root(2, t)
            moe(1)

        @block.vector
        def _(dve):
            own = Steps(dve, sem("dve_steps"))
            V = nc.vector

            def layer_norm(n, t, y_made):
                x, r, halves = x_tok[:, t], LN_NORM[n][:, t], (slice(0, 512), slice(512, 1024))
                if n == 0 and t == 0:
                    dve.wait_ge(sem("x_in"), 16)
                src = []
                for half, hs in enumerate(halves):
                    y_made(t, half)
                    y = bank[LN_BANKS[n][t][half]][:, :]
                    if n % 2 == 0:
                        own.did(V.scalar_tensor_tensor(out=r[:, hs], in0=x[:, hs], scalar=ALPHA, in1=y,
                                                       op0=ALU.mult, op1=ALU.add))
                        own.settle()
                    src.append(y if n % 2 else r[:, hs])
                    own.did(V.bn_stats(stats[:, t, half], src[half]))
                own.settle()
                V.bn_aggr(mean_var[:, t], stats[:, t]).then_inc(sem("ln_var"), 1)
                dve.wait_ge(sem("ln_var"), TC * n + t + 1)
                if t == 0:
                    dve.wait_ge(sem("ln_gb_in"), 16 * (n + 1))
                for half, hs in enumerate(halves):
                    own.did(V.scalar_tensor_tensor(out=r[:, hs], in0=src[half], scalar=mean_var[:, t, 0:1],
                                                   in1=ln_gb[:, 0, hs], op0=ALU.subtract, op1=ALU.mult))
                dve.wait_ge(sem("ln_root"), TC * n + t + 1)
                own.did(V.reciprocal(rstd[:, t:t + 1], rstd[:, t:t + 1]))
                own.settle()
                for hs in halves:
                    V.scalar_tensor_tensor(out=x[:, hs], in0=r[:, hs], scalar=rstd[:, t:t + 1], in1=ln_gb[:, 1, hs],
                                           op0=ALU.mult, op1=ALU.add).then_inc(sem("ln_done"), 1)

            dve.wait_ge(sem("pos_in"), 16)
            dve.wait_ge(sem("cols_in"), 16)
            own.did(V.tensor_copy(A.posf, A.ang.bitcast(I32)))
            own.settle()
            own.did(V.tensor_scalar(A.ang, A.posf, cols[:, COL_INVF:COL_INVF + 1], None, ALU.mult))
            own.settle()
            own.did(V.tensor_scalar(A.turns[:, 0], A.ang, 1.0 / TWO_PI, MAGIC, ALU.mult, ALU.add))
            own.settle()
            own.did(V.tensor_scalar(A.turns[:, 1], A.turns[:, 0], MAGIC, None, ALU.subtract))
            own.settle()
            for part in (PI_A, PI_B, PI_C):
                own.did(V.scalar_tensor_tensor(out=A.ang, in0=A.turns[:, 1], scalar=-part, in1=A.ang,
                                               op0=ALU.mult, op1=ALU.add))
                own.settle()
            V.tensor_scalar(A.turns[:, 0], A.ang, 3.1415925, -3.1415925, ALU.min, ALU.max
                            ).then_inc(sem("ang_ready"), 1)
            for t in range(TC):
                dve.wait_ge(sem("c_ready"), t + 1)
                own.did(V.tensor_copy(A.kr[:, t], bank[2 + t][:, 0:ROPE].rearrange("p (b f) -> p b f", b=2)
                                      .unsqueeze(2).broadcast_to([P, 2, HEADS_PER_ROPE, HALF])))
                dve.wait_ge(sem("c_root"), t + 1)
                own.did(V.reciprocal(A.rs[:, t], A.rs[:, t]))
                own.settle()
                for part in range(2):
                    ch = slice(part * 256, part * 256 + 256)
                    V.tensor_scalar(A.cn[:, t, ch], bank[t][:, ch], A.rs[:, t, part:part + 1], None, ALU.mult
                                    ).then_inc(sem("cn_ready"), 1)
            dve.wait_ge(sem("cT_ready"), 1)
            for k in range(RC):
                V.tensor_scalar(A.cqT[:, k], bank[4][:, k * S:(k + 1) * S], cols[:, COL_GQ + k:COL_GQ + k + 1], None,
                                ALU.mult).then_inc(sem("cqT_ready"), 1)
            dve.wait_ge(sem("rope_ready"), 1)

            def rotate(src):
                ab = src.rearrange("p (b s) -> p b s", b=2)
                own.did(V.tensor_tensor(A.rt[:, 0], ab, A.cos.unsqueeze(1).broadcast_to([P, 2, S]), ALU.mult))
                return V.tensor_tensor(A.rt[:, 1], ab, A.sin.unsqueeze(1).broadcast_to([P, 2, S]), ALU.mult)

            def rotated(dst):
                own.did(V.tensor_tensor(dst[:, 0], A.rt[:, 0, 0], A.rt[:, 1, 1], ALU.subtract))
                return V.tensor_tensor(dst[:, 1], A.rt[:, 0, 1], A.rt[:, 1, 0], ALU.add)

            own.did(rotate(bank[6][:, :]))
            own.settle()
            rotated(A.kpe).then_inc(sem("kpe_ready"), 1)
            dve.wait_ge(sem("kpe_ready"), 1)
            n_by_dve = 0
            for i, (what, j) in enumerate(PROJ):
                if i % 2 == 0:
                    continue
                dve.wait_ge(sem("proj_made"), i + 1)
                n_by_dve += 1
                src = bank[i % 4][:, :]
                if what == "qpe":
                    own.settle()
                    rotate(src).then_inc(sem("proj_by_dve"), 1)
                    dve.wait_ge(sem("proj_by_dve"), n_by_dve)
                    own.settle()
                    rotated(A.qpe[:, j]).then_inc(sem("rotated"), 1)
                    dve.wait_ge(sem("rotated"), j + 1)
                elif what == "v":
                    V.tensor_copy(A.val[:, j // 2, (j % 2) * 512:(j % 2) * 512 + 512], src
                                  ).then_inc(sem("proj_by_dve"), 1)
                else:
                    V.tensor_copy((A.qn if what == "qn" else A.kn)[:, 2 * j:2 * j + 2],
                                  src.rearrange("p (a s) -> p a s", a=2)).then_inc(sem("proj_by_dve"), 1)

            for i in range(HEADS + 2):
                if 1 <= i <= HEADS:
                    h = i - 1
                    dve.wait_ge(sem("exp_ready"), 2 * i)
                    own.did(V.reciprocal(A.rc[:, h], A.sm[:, h]))
                    own.settle()
                    for b, (lo, hi) in enumerate(((0, 128), (128, 384))):
                        V.tensor_scalar(A.p[:, h % 2, lo:hi], A.p[:, h % 2, lo:hi], A.rc[:, h, b:b + 1], None, ALU.mult
                                        ).then_inc(sem("p_ready"), 1)
                if i < HEADS:
                    dve.wait_ge(sem("s_made"), i + 1)
                    for b, (lo, hi) in enumerate(((0, 128), (128, 384))):
                        own.did(V.tensor_reduce(A.mx[:, i, b:b + 1], bank[i % 2][:, lo:hi], AX.X, ALU.max))
                    own.settle()
                    V.tensor_scalar(A.nm[:, i], A.mx[:, i], -SCALE, None, ALU.mult).then_inc(sem("max_ready"), 1)
                if i >= 2:
                    h = i - 2
                    dve.wait_ge(sem("o_made"), h + 1)
                    V.tensor_copy(A.oT[:, h], bank[4 + h % 2][:, 0:S]).then_inc(sem("oT_ready"), 1)

            for t in range(TC):
                layer_norm(0, t, lambda t, half: dve.wait_ge(sem("y_ready"), 2 * t + half + 1))

            def moe(layer):
                s = f"moe{layer}_"
                ln = 2 * layer + 1
                if layer == 0:
                    dve.wait_ge(sem("small_in"), 16 * 5)
                own.did(V.memset(E.posm_all[:, :, MAX_ROUNDS * EXPERTS:], FAR))
                own.did(V.memset(E.gate_all[:, :, MAX_ROUNDS * EXPERTS:], 0.0))
                for r in range(MAX_ROUNDS):
                    own.did(V.memset(E.full_rounds[:, r:r + 1], float(SLOTS * (r + 1)) if r < MAX_ROUNDS - 1 else FAR))
                dve.wait_ge(sem("scores"), layer + 1)
                own.did(V.tensor_tensor(E.sel, E.sc, router_b[:, :].unsqueeze(1).broadcast_to([P, TC, EXPERTS]),
                                        ALU.add))
                own.settle()

                def ranks(values, n, dst):
                    full = [P, n, PER_GROUP, PER_GROUP]
                    vj = values.unsqueeze(3).broadcast_to(full)
                    vk = values.unsqueeze(2).broadcast_to(full)
                    above, tied = E.above[:, 0:n], E.tied[:, 0:n]
                    own.did(V.tensor_tensor(above, vk, vj, ALU.subtract))
                    own.settle()
                    own.did(V.scalar_tensor_tensor(
                        out=tied.rearrange("p n j k -> p n (j k)"), in0=above.rearrange("p n j k -> p n (j k)"),
                        scalar=0.0, in1=lower[:, :, :].rearrange("p j k -> p (j k)").unsqueeze(1)
                        .broadcast_to([P, n, PER_GROUP * PER_GROUP]), op0=ALU.is_equal, op1=ALU.mult))
                    own.settle()
                    own.did(V.scalar_tensor_tensor(
                        out=above.rearrange("p n j k -> p (n j k)"), in0=above.rearrange("p n j k -> p (n j k)"),
                        scalar=0.0, in1=tied.rearrange("p n j k -> p (n j k)"), op0=ALU.is_gt, op1=ALU.add))
                    own.settle()
                    own.did(V.tensor_reduce(dst, above, AX.X, ALU.add))
                    own.settle()

                def by_group(v):
                    return v.rearrange("p t (g j) -> p (t g) j", j=PER_GROUP)

                ranks(by_group(E.sel), TC * GROUPS, by_group(E.rank))
                own.did(V.scalar_tensor_tensor(out=E.top_sel, in0=E.rank, scalar=1.5, in1=E.sel,
                                               op0=ALU.is_lt, op1=ALU.mult))
                own.did(V.tensor_scalar(E.top, E.rank, 1.5, None, ALU.is_lt))
                own.settle()
                own.did(V.tensor_reduce(E.gsum.rearrange("p t g -> p (t g)"), by_group(E.top_sel), AX.X, ALU.add))
                own.settle()
                ranks(E.gsum, TC, E.grank)
                V.scalar_tensor_tensor(
                    out=by_group(E.mask), in0=E.grank.rearrange("p t g -> p (t g)").unsqueeze(2)
                    .broadcast_to([P, TC * GROUPS, PER_GROUP]), scalar=0.5, in1=by_group(E.top),
                    op0=ALU.is_lt, op1=ALU.mult).then_inc(sem("mask_ready"), 1)
                dve.wait_ge(sem("mask_ready"), layer + 1)
                own.did(V.tensor_tensor(E.gate, E.mask, E.sc, ALU.mult))
                own.settle()
                own.did(V.tensor_reduce(E.den, E.gate, AX.X, ALU.add))
                own.settle()
                own.did(V.reciprocal(E.rden, E.den))
                own.settle()
                own.did(V.tensor_tensor(E.gate, E.gate, E.rden.unsqueeze(2).broadcast_to([P, TC, EXPERTS]), ALU.mult))
                own.settle()
                for r in range(MAX_ROUNDS):
                    own.did(V.tensor_copy(E.gate_all[:, :, r * EXPERTS:(r + 1) * EXPERTS], E.gate))

                def one_hot(g):
                    V.tensor_tensor(
                        E.oh, slot_no[:, :].unsqueeze(1).unsqueeze(1).broadcast_to([P, TC, 2, SLOTS]),
                        E.posm_all[:, :, bass.ds(g * 2, 2)].unsqueeze(3).broadcast_to([P, TC, 2, SLOTS]),
                        ALU.is_equal).then_inc(sem(s + "oh"), 1)

                def gathered(count):
                    dve.wait_ge(sem(s + "gathered"), count)
                    V.tensor_copy(E.xg[:, 0:4], bank[6][:, :].rearrange("p (k s) -> p k s", k=4)
                                  ).then_inc(sem(s + "xg_by_dve"), 1)

                dve.wait_ge(sem("places"), layer + 1)
                places = bank[7][:, 0:TC * EXPERTS].rearrange("p (t e) -> p t e", t=TC)
                own.did(V.scalar_tensor_tensor(out=E.posm, in0=places, scalar=-FAR, in1=E.mask,
                                               op0=ALU.add, op1=ALU.mult))
                own.did(V.tensor_reduce(E.most, bank[7][:, 64:64 + EXPERTS], AX.X, ALU.max))
                own.settle()
                for r in range(MAX_ROUNDS):
                    own.did(V.tensor_scalar(E.posm_all[:, :, r * EXPERTS:(r + 1) * EXPERTS], E.posm, FAR - SLOTS * r,
                                            None, ALU.add))
                own.settle()
                one_hot(0)
                own.did(V.tensor_scalar(E.over, E.full_rounds, E.most, float(PAIRS), ALU.is_lt, ALU.mult))
                own.settle()
                own.did(V.tensor_reduce(E.nrounds, E.over, AX.X, ALU.add))
                own.settle()
                V.tensor_copy(extra_pairs_at[:, layer:layer + 1], E.nrounds).then_inc(sem(f"moe{layer}_rounds"), 1)
                gathered(1)
                dve.wait_ge(sem(f"moe{layer}_rounds"), 1)
                extra = extra_pairs(dve, layer)
                with dve.Fori(0, extra + PAIRS) as g:
                    dve.wait_ge(sem(s + "gates_turned"), g + 1)
                    V.tensor_copy(E.gt_sb, bank[6][:, 0:S].rearrange("p (t n) -> p t n", t=TC)
                                  ).then_inc(sem(s + "gates"), 1)
                    one_hot(g + 1)
                    dve.wait_ge(sem(s + "silu"), g + 1)
                    V.tensor_tensor(E.h, E.sg, bank[5][:, :], ALU.mult).then_inc(sem(s + "h"), 1)
                    gathered(g + 2)
                    dve.wait_ge(sem(s + "used"), g * RING + DC + 2)
                    V.tensor_copy(E.ye[:, 0], bank[5][:, :]).then_inc(sem(s + "ye0"), 1)
                for t in range(TC):
                    layer_norm(ln, t, lambda t, half: dve.wait_ge(sem(s + "added"), extra * (2 * TC) + PAIRS * 2 * TC))

            moe(0)

            V.memset(M.xm[:, :, 0:TAPS - 1], 0.0).then_inc(sem("pads"), 1)
            for c in range(IC + 2):
                if c < IC:
                    dve.wait_ge(sem("xm_ready"), c + 1)
                    if c >= 2:
                        dve.wait_ge(sem("xc_ready"), c - 1)
                    x = M.xm[:, c % 4]
                    w = COL_CONVW + c * TAPS
                    ping, pong = M.cv[:, c % 2], M.cv2[:, c % 2]
                    own.did(V.tensor_scalar(pong, x[:, 0:S], cols[:, w:w + 1],
                                            cols[:, COL_CONVB + c:COL_CONVB + c + 1], ALU.mult, ALU.add))
                    own.settle()
                    for tap in range(1, TAPS):
                        src, dst = (pong, ping) if tap % 2 else (ping, pong)
                        last = V.scalar_tensor_tensor(out=dst, in0=x[:, tap:tap + S],
                                                      scalar=cols[:, w + tap:w + tap + 1],
                                                      in1=src, op0=ALU.mult, op1=ALU.add)
                        if tap < TAPS - 1:
                            own.did(last)
                            own.settle()
                    last.then_inc(sem("conv_done"), 1)
                if c >= 2:
                    d = c - 2
                    dve.wait_ge(sem("qkv_made"), d + 1)
                    if d >= 2:
                        dve.wait_ge(sem("scored"), d - 1)
                    V.tensor_copy(M.qk[:, d % 2], bank[2 + d % 2][:, :].rearrange("p (a s) -> p a s", a=2)
                                  ).then_inc(sem("qk_ready"), 1)
                if c >= 3 and (c - 3) % CPH == CPH - 1 or c == IC + 1:
                    h = (c - 3) // CPH if c <= IC else M_HEADS - 1
                    dve.wait_ge(sem("scored"), (h + 1) * CPH)
                    V.tensor_scalar(M.p[:, h], bank[6][:, 0:384], HD ** -0.5, None, ALU.mult
                                    ).then_inc(sem("s_taken"), 1)
            dve.wait_ge(sem("v_ready"), IC)
            own.did(V.tensor_reduce(M.gv, M.val[:, :, :, P:].rearrange("p t c n -> p t n c"), AX.X, ALU.add))
            own.settle()
            own.did(V.tensor_tensor(M.gv, M.gv, bank[7][:, 0:16].rearrange("p (t n) -> p t n", t=TC), ALU.add))
            own.settle()
            own.did(V.tensor_tensor(M.pre, M.gv, gate_b[:, :].unsqueeze(1).broadcast_to([P, TC, 2 * M_HEADS]), ALU.add))
            own.settle()
            V.tensor_scalar(M.lf, M.pre[:, :, M_HEADS:], 0.0, None, ALU.min).then_inc(sem("pre_ready"), 1)
            dve.wait_ge(sem("log_ready"), 1)
            V.tensor_tensor(M.lf, M.lf, M.fa, ALU.subtract).then_inc(sem("lf_ready"), 1)
            dve.wait_ge(sem("b_made"), 1)
            b_psum = bank[2][:, 0:TC * M_HEADS].rearrange("p (t n) -> p t n", t=TC)
            own.did(V.tensor_copy(M.b, b_psum))
            V.tensor_tensor(M.aa, M.pre[:, :, 0:M_HEADS], b_psum, ALU.subtract).then_inc(sem("a_ready"), 1)
            own.did(V.memset(M.mrow[0:M_HEADS, :, 0:P], 0.0))
            dve.wait_ge(sem("a_turned"), 1)
            own.did(V.tensor_scalar(M.mrow[0:M_HEADS, 0, P:], bank[3][0:M_HEADS, 0:S], 0.0, None, ALU.max))
            own.settle()
            shift, cur, doublings = 1, 0, 0
            while shift < S:
                V.tensor_tensor(M.mrow[0:M_HEADS, 1 - cur, P:], M.mrow[0:M_HEADS, cur, P:],
                                M.mrow[0:M_HEADS, cur, P - shift:P + S - shift], ALU.max
                                ).then_inc(sem("max_row"), 1)
                shift, cur, doublings = shift * 2, 1 - cur, doublings + 1
                dve.wait_ge(sem("max_row"), doublings)
            assert cur == 0 and doublings == DOUBLINGS
            dve.wait_ge(sem("max_spread"), 1)
            V.tensor_tensor(M.mt, M.b, bank[2][:, 0:TC * M_HEADS].rearrange("p (t n) -> p t n", t=TC), ALU.add
                            ).then_inc(sem("m_ready"), 1)
            for h in range(M_HEADS):
                far = bank[4 + h // 2][:, (h % 2) * S:(h % 2) * S + S]
                if h:
                    dve.wait_ge(sem("decay_ready"), h)
                own.did(V.tensor_scalar(M.ar[:, 0:S], far, M.aa[:, 0, h:h + 1], 0.0, ALU.subtract, ALU.max))
                V.tensor_scalar(M.ar[:, S:S + P], far[:, P:S], M.aa[:, 1, h:h + 1], 0.0, ALU.subtract, ALU.max
                                ).then_inc(sem("reach_ready"), 1)
                dve.wait_ge(sem("decay_ready"), h + 1)
                own.did(V.tensor_tensor(M.p[:, h], M.p[:, h], M.er, ALU.mult))
                own.settle()
                own.did(V.tensor_tensor(M.p[:, h, 0:P], M.p[:, h, 0:P], upto[:, :], ALU.mult))
                V.tensor_tensor(M.p[:, h, S:S + P], M.p[:, h, S:S + P], upto[:, :], ALU.mult
                                ).then_inc(sem("w_ready"), 1)
            dve.wait_ge(sem("em_ready"), 1)
            for h in range(M_HEADS):
                dve.wait_ge(sem("num_made"), h + 1)
                own.did(V.tensor_scalar(M.dm, bank[4][:, 2 * h:2 * h + 2], -1.0, None, ALU.mult))
                own.did(V.tensor_tensor(M.dn, bank[4][:, 2 * h:2 * h + 2], M.em[:, :, h], ALU.max))
                for t in range(TC):
                    own.did(V.bn_stats(M.st[:, t], bank[2 + t][:, :]))
                own.settle()
                own.did(V.tensor_tensor(M.dn, M.dn, M.dm, ALU.max))
                for t in range(TC):
                    own.did(V.bn_aggr(M.mv[:, t], M.st[:, t]))
                own.settle()
                own.did(V.reciprocal(M.rd, M.dn))
                own.settle()
                own.did(V.tensor_tensor(M.w2, M.mv[:, :, 1], M.rd, ALU.mult))
                own.settle()
                V.tensor_tensor(M.w2, M.w2, M.rd, ALU.mult).then_inc(sem("h_var"), 1)
                dve.wait_ge(sem("h_root"), h + 1)
                own.did(V.reciprocal(M.w1, M.w1))
                own.settle()
                own.did(V.tensor_tensor(M.w1, M.w1, M.rd, ALU.mult))
                own.settle()
                if h >= 2:
                    dve.wait_ge(sem("hn_turned"), 2 * (h - 1))
                for t in range(TC):
                    V.tensor_scalar(M.hn[:, t, (h % 2) * HD:(h % 2) * HD + HD], bank[2 + t][:, :], M.mv[:, t, 0:1],
                                    M.w1[:, t:t + 1], ALU.subtract, ALU.mult).then_inc(sem("hn_ready"), 1)
                for j in range(2):
                    dve.wait_ge(sem("hn_turned"), 2 * h + j + 1)
                    for cc in range(2):
                        c = h * CPH + 2 * j + cc
                        V.scalar_tensor_tensor(
                            out=M.sxc[:, c], in0=bank[5][:, cc * S:(cc + 1) * S],
                            scalar=cols[:, COL_GOUT + c:COL_GOUT + c + 1],
                            in1=M.sxc[:, c], op0=ALU.mult, op1=ALU.add).then_inc(sem("hT_taken"), 1)
            for t in range(TC):
                layer_norm(2, t, lambda t, half: dve.wait_ge(sem("y_ready"), 4 + 2 * t + half + 1))
            moe(1)

        @block.tensor
        def _(pe):
            mm = nc.tensor.matmul

            for t in range(TC):
                for k in range(DC):
                    if t == 0 and k % 2 == 0:
                        pe.wait_ge(sem(f"x_w_in{k // 2}"), 32)
                    xk = xT[:, k, t * P:(t + 1) * P]
                    mm(bank[t][:, :], xk, win[:, k, 0:512], start=(k == 0), stop=(k == DC - 1))
                    last = mm(bank[2 + t][:, 0:ROPE], xk, win[:, k, 512:576], start=(k == 0), stop=(k == DC - 1))
                last.then_inc(sem("c_ready"), 1)
            pe.wait_ge(sem("consts"), 1)
            for t in range(TC):
                pe.wait_ge(sem("cn_ready"), 2 * t + 2)
                for k in range(RC):
                    nc.tensor.transpose(bank[4][:, k * S + t * P:k * S + t * P + P], A.cn[:, t, k * P:(k + 1) * P],
                                        ident[:, :])
                    nc.tensor.transpose(bank[5][:, k * S + t * P:k * S + t * P + P],
                                        A.cn[:, t, 256 + k * P:256 + (k + 1) * P], ident[:, :])
                    last = nc.tensor.transpose(bank[6][:, k * S + t * P:k * S + t * P + P],
                                               A.kr[:, t, k].rearrange("p r f -> p (r f)"), ident[:, :])
            last.then_inc(sem("cT_ready"), 1)

            pe.wait_ge(sem("w_uq_in"), 16)
            pe.wait_ge(sem("w_ukv_in"), 16)
            pe.wait_ge(sem("cqT_ready"), 2)
            for i, (what, j) in enumerate(PROJ):
                if i >= 4:
                    pe.wait_ge(sem("proj_by_act" if i % 2 == 0 else "proj_by_dve"), (i - 4) // 2 + 1)
                if (what, j) == ("kn", 0):
                    pe.wait_ge(sem("ckvT_ready"), 2)
                out_bank = bank[i % 4]
                if what == "v":
                    t, n = divmod(j, 2)
                    for k in range(RC):
                        last = mm(out_bank[:, :], A.ckvT[:, k, t * P:(t + 1) * P],
                                  wukv[:, k, 1024 + n * 512:1024 + n * 512 + 512], start=(k == 0), stop=(k == RC - 1))
                else:
                    w, base, rhs = {"qn": (wuq, 0, A.cqT), "qpe": (wuq, 1024, A.cqT), "kn": (wukv, 0, A.ckvT)}[what]
                    for b in range(2):
                        col = base + (2 * j + b) * P
                        for k in range(RC):
                            last = mm(out_bank[:, b * S:(b + 1) * S], w[:, k, col:col + P], rhs[:, k],
                                      start=(k == 0), stop=(k == RC - 1))
                last.then_inc(sem("proj_made"), 1)

            pe.wait_ge(sem("rotated"), HEADS // HEADS_PER_ROPE)
            pe.wait_ge(sem("kpe_of_ready"), HEADS_PER_ROPE)
            pe.wait_ge(sem("proj_by_act"), len(PROJ) // 2)
            pe.wait_ge(sem("proj_by_dve"), len(PROJ) // 2)
            for i in range(HEADS + 2):
                if i < HEADS:
                    grp, j = divmod(i, HEADS_PER_ROPE)
                    if i >= 2:
                        pe.wait_ge(sem("exp_ready"), 2 * (i - 1))
                    for q, (lo, n) in enumerate(((0, P), (P, S))):
                        dst, qs = bank[i % 2][:, lo:lo + n], slice(q * P, (q + 1) * P)
                        mm(dst, A.qn[:, i, qs], A.kn[:, i, 0:n], start=True, stop=False, skip_group_check=True)
                        for b in range(2):
                            mm(dst, A.qpe[:, grp, b, qs], A.kpe_of[:, j, b, 0:n], start=False, stop=False,
                               skip_group_check=True)
                        last = mm(bank[i % 2][:, lo + n - P:lo + n], ident_bf[:, :], causal_bf[:, :], start=False,
                                  stop=True, skip_group_check=True)
                    last.then_inc(sem("s_made"), 1)
                if 1 <= i <= HEADS:
                    h = i - 1
                    pe.wait_ge(sem("p_ready"), 2 * i)
                    if h >= 2:
                        pe.wait_ge(sem("pT_ready"), h - 1)
                    for b, col in enumerate((0, P, S)):
                        last = nc.tensor.transpose(bank[2 + h % 2][:, col:col + P], A.p[:, h % 2, col:col + P],
                                                   ident[:, :])
                    last.then_inc(sem("p_turned"), 1)
                if i >= 2:
                    h = i - 2
                    pe.wait_ge(sem("pT_ready"), h + 1)
                    if h >= 2:
                        pe.wait_ge(sem("oT_ready"), h - 1)
                    vs = slice(h * P, (h + 1) * P)
                    mm(bank[4 + h % 2][:, 0:S], A.val[:, 0, vs], A.pT[:, h % 2, 0:S], start=True, stop=False,
                       skip_group_check=True)
                    mm(bank[4 + h % 2][:, P:S], A.val[:, 1, vs], A.pT[:, h % 2, S:384], start=False, stop=True,
                       skip_group_check=True).then_inc(sem("o_made"), 1)

            pe.wait_ge(sem("w_o_in"), 16)
            pe.wait_ge(sem("oT_ready"), HEADS)
            for t in range(TC):
                for half in range(2):
                    for h in range(HEADS):
                        last = mm(bank[LN.mla[t][half]][:, :], A.oT[:, h, t * P:(t + 1) * P],
                                  wo[:, h, half * 512:half * 512 + 512], start=(h == 0), stop=(h == HEADS - 1))
                    last.then_inc(sem("y_ready"), 1)

            def turn_x(n):
                for t in range(TC):
                    for k in range(DC):
                        if k % 4 == 0:
                            pe.wait_ge(sem("ln_done"), n * LN_STEPS + 2 * t + k // 4 + 1)
                        last = nc.tensor.transpose(bank[TURN_BANKS[t] + k // 4][:, (k % 4) * P:(k % 4) * P + P],
                                                   x_tok[:, t, k * P:(k + 1) * P], ident[:, :])
                        if k % 4 == 3:
                            last.then_inc(sem("xT_made"), 1)

            def moe(layer):
                s = f"moe{layer}_"
                turn_x(2 * layer)
                if layer == 0:
                    pe.wait_ge(sem("small_in"), 16 * 5)
                pe.wait_ge(sem("xT_ready"), (4, 12)[layer])
                for t in range(TC):
                    for k in range(DC):
                        last = mm(bank[6][:, t * EXPERTS:(t + 1) * EXPERTS], xT[:, k, t * P:(t + 1) * P],
                                  router_w[:, k, :], start=(k == 0), stop=(k == DC - 1))
                last.then_inc(sem("logits"), 1)
                for t in range(TC):
                    for half in range(2):
                        mm(bank[LN.moe[t][half]][:, :], alpha_ident[:, :], x_tok[:, t, half * 512:half * 512 + 512],
                           start=True, stop=False, skip_group_check=True)
                pe.wait_ge(sem("mask_ready"), layer + 1)
                mm(bank[7][:, 0:16], before[:, :], E.mask[:, 0], start=True, stop=True)
                mm(bank[7][:, 16:32], before[:, :], E.mask[:, 1], start=True, stop=False)
                mm(bank[7][:, 16:32], ones[:, :], E.mask[:, 0], start=False, stop=True)
                mm(bank[7][:, 64:80], ones[:, :], E.mask[:, 0], start=True, stop=False)
                mm(bank[7][:, 64:80], ones[:, :], E.mask[:, 1], start=False, stop=True).then_inc(sem("places"), 1)
                def gather():
                    for k in range(DC):
                        for i in range(3 * TC):
                            part, t = divmod(i, TC)
                            last = mm(bank[6 + k // 4][:, (k % 4) * P:(k % 4) * P + P],
                                      E.parts[:, part, t, k * P:(k + 1) * P],
                                      E.oh[:, t].rearrange("p a s -> p (a s)"), start=(i == 0), stop=(i == 3 * TC - 1))
                    last.then_inc(sem(s + "gathered"), 1)

                pe.wait_ge(sem("x_part2"), (layer + 1) * TC)
                pe.wait_ge(sem(s + "oh"), 1)
                gather()
                pe.wait_ge(sem(f"moe{layer}_rounds"), 1)
                extra = extra_pairs(pe, layer)
                side = (slice(0, SLOTS), slice(SLOTS, 2 * SLOTS))
                with pe.Fori(0, extra + PAIRS) as g:
                    pe.wait_ge(sem(s + "ohg"), g + 1)
                    pe.wait_ge(sem(s + "xg_by_dve"), g + 1)
                    for t in range(TC):
                        last = nc.tensor.transpose(bank[6][:, t * P:(t + 1) * P],
                                                   E.ohg[:, t].rearrange("p a s -> p (a s)"), ident[:, :])
                    last.then_inc(sem(s + "gates_turned"), 1)
                    pe.wait_ge(sem(s + "xg_by_act"), g + 1)
                    for k in range(DC):
                        pe.wait_ge(sem(LANDED[layer].format(k)), g * 16 + 16 + LANDED_BEFORE[layer])
                        w = slot(k).rearrange("p (m a f) -> p m a f", m=2, a=2)
                        for m in range(2):
                            for e in range(2):
                                last = mm(bank[4 + m][side[e], :], E.xg[:, k, side[e]], w[:, m, e],
                                          start=(k == 0), stop=(k == DC - 1), skip_group_check=True)
                        last.then_inc(sem(s + "used"), 1)
                    pe.wait_ge(sem(s + "oh"), g + 2)
                    pe.wait_ge(sem(s + "gates"), g + 1)
                    gather()
                    pe.wait_ge(sem(s + "h"), g + 1)
                    for f in range(FC):
                        last = nc.tensor.transpose(bank[4][:, f * P:(f + 1) * P], E.h[:, f * P:(f + 1) * P],
                                                   ident[:, :])
                    last.then_inc(sem(s + "h_turned"), 1)
                    pe.wait_ge(sem(s + "hT"), g + 1)
                    for half in range(2):
                        for j in range(2):
                            u = DC + 2 * half + j
                            pe.wait_ge(sem(LANDED[layer].format(u)), g * 16 + 16 + LANDED_BEFORE[layer])
                            w = slot(u).rearrange("p (f a n) -> p f a n", f=2, a=2)
                            for ff in range(2):
                                for e in range(2):
                                    f = 2 * j + ff
                                    last = mm(bank[5 - half][side[e], :], E.hT[:, f, side[e]], w[:, ff, e],
                                              start=(f == 0), stop=(f == FC - 1), skip_group_check=True)
                            last.then_inc(sem(s + "used"), 1)
                    for half in range(2):
                        pe.wait_ge(sem(s + f"ye{half}"), g + 1)
                        for t in range(TC):
                            mm(bank[LN.moe[t][half]][:, :], E.gt_sb[:, t], E.ye[:, half], start=False, stop=False,
                               skip_group_check=True).then_inc(sem(s + "added"), 1)

            moe(0)

            turn_x(1)
            pe.wait_ge(sem("xT_ready"), 2 * 2 * TC)

            def unit_landed(u):
                pe.wait_ge(sem(LANDED[1].format(u % RING)), 16 * (u // RING + 1))

            def inner(c, out_bank, name):
                if c % 2 == 0:
                    unit_landed(c // 2)
                w = slot(c // 2 % RING).rearrange("p (c k n) -> p c k n", c=2, k=DC)
                for k in range(DC):
                    last = mm(out_bank[:, 0:S], w[:, c % 2, k], xT[:, k], start=(k == 0), stop=(k == DC - 1))
                last.then_inc(sem(name), 1)

            for i in range(IC + 3):
                if i < IC:
                    if i >= 2:
                        pe.wait_ge(sem("xm_ready"), i - 1)
                    inner(i, bank[i % 2], "xm_made")
                if 2 <= i <= IC + 1:
                    c = i - 2
                    pe.wait_ge(sem("w3_made"), c + 1)
                    pe.wait_ge(sem("xc_ready"), c + 1)
                    if c >= 2:
                        pe.wait_ge(sem("qk_ready"), c - 1)
                        pe.wait_ge(sem("v_ready"), c - 1)
                    if c == 0:
                        pe.wait_ge(sem("gate_w_made"), 1)
                    w3, xc, xm = M.w3[:, c % 2], M.xc[:, c % 3], M.xm[:, c % 4, TAPS - 1:]
                    mm(bank[2 + c % 2][:, 0:S], w3[:, 0:P], xc, start=True, stop=True)
                    mm(bank[2 + c % 2][:, S:], w3[:, P:2 * P], xc, start=True, stop=True)
                    for t in range(TC):
                        mm(bank[7][:, t * 8:t * 8 + 8], xc[:, t * P:(t + 1) * P], gate_qk[:, c],
                           start=(c == t == 0), stop=False, skip_group_check=True)
                    for t in range(TC):
                        last = mm(bank[4 + c % 2][:, t * V_COLS:(t + 1) * V_COLS], xm[:, t * P:(t + 1) * P],
                                  w3[:, 2 * P:], start=True, stop=True)
                    last.then_inc(sem("qkv_made"), 1)
                if i >= 3:
                    c = i - 3
                    pe.wait_ge(sem("qk_ready"), c + 1)
                    q, k = M.qk[:, c % 2, 0], M.qk[:, c % 2, 1]
                    h, first = divmod(c, CPH)
                    if h and first == 0:
                        pe.wait_ge(sem("s_taken"), h)
                    mm(bank[6][:, 0:S], k[:, 0:P], q, start=(first == 0), stop=False, skip_group_check=True)
                    mm(bank[6][:, S:S + P], k[:, P:S], q[:, P:S], start=False, stop=False, skip_group_check=True
                       ).then_inc(sem("scored"), 1)

            def z(c):
                if c < 2:
                    pe.wait_ge(sem("xm_ready"), IC)
                else:
                    pe.wait_ge(sem("z_ready"), c - 1)
                inner(IC + c, bank[c % 2], "z_made")

            for c in range(4):
                z(c)
            pe.wait_ge(sem("lf_ready"), 1)
            mm(bank[2][:, 0:4], upto[:, :], M.lf[:, 0], start=True, stop=True)
            mm(bank[2][:, 4:8], upto[:, :], M.lf[:, 1], start=True, stop=False)
            mm(bank[2][:, 4:8], ones[:, :], M.lf[:, 0], start=False, stop=True).then_inc(sem("b_made"), 1)
            z(4)
            pe.wait_ge(sem("a_ready"), 1)
            for t in range(TC):
                last = mm(bank[3][0:M_HEADS, t * P:(t + 1) * P], M.aa[:, t], ident[:, :], start=True, stop=True)
            last.then_inc(sem("a_turned"), 1)
            for c in range(5, 8):
                z(c)
            pe.wait_ge(sem("max_row"), DOUBLINGS)
            row = M.mrow[0:M_HEADS, 0, P:]
            for h in range(M_HEADS):
                mm(bank[4 + h // 2][:, (h % 2) * S:(h % 2) * S + S], head_row[:, h, :], row, start=True, stop=True)
            for t in range(TC):
                last = mm(bank[2][:, t * 4:t * 4 + 4], row[:, t * P:(t + 1) * P], ident[0:M_HEADS, 0:M_HEADS],
                          start=True, stop=True)
            last.then_inc(sem("max_spread"), 1)
            for c in range(8, 12):
                z(c)

            def head(h):
                pe.wait_ge(sem("w_ready"), max(2, h + 1))
                if h:
                    pe.wait_ge(sem("hn_ready"), TC * h)
                else:
                    pe.wait_ge(sem("em_ready"), 1)
                if h == 0:
                    pe.wait_ge(sem("v_ready"), IC)
                w = M.p[:, h]
                products = ((0, w[:, 0:P], 0, True, True), (1, w[:, P:S], 0, True, False),
                            (1, w[:, S:S + P], 1, False, True))
                for t, lhs, key, start, stop in products:
                    mm(bank[4][:, 2 * h + t:2 * h + t + 1], lhs, ones[:, 0:1], start=start, stop=stop)
                for t, lhs, key, start, stop in products:
                    last = mm(bank[2 + t][:, :], lhs, M.val[:, key, h * CPH:(h + 1) * CPH, 0:P], start=start, stop=stop)
                last.then_inc(sem("num_made"), 1)

            def turn(h, j):
                pe.wait_ge(sem("hn_ready"), TC * (h + 1))
                if h == j == 0:
                    pe.wait_ge(sem("reach_ready"), M_HEADS)
                else:
                    pe.wait_ge(sem("hT_taken"), 2 * (2 * h + j))
                for cc in range(2):
                    ch = (h % 2) * HD + (2 * j + cc) * P
                    for t in range(TC):
                        last = nc.tensor.transpose(bank[5][:, cc * S + t * P:cc * S + t * P + P],
                                                   M.hn[:, t, ch:ch + P], ident[:, :])
                last.then_inc(sem("hn_turned"), 1)

            def way_out(h):
                if h == 0:
                    pe.wait_ge(sem("z_ready"), IC)
                    pe.wait_ge(sem("s_taken"), M_HEADS)
                for j in range(CPH // 2):
                    unit_landed(IC + h * CPH // 2 + j)
                for t in range(TC):
                    for half in range(2):
                        for c in range(h * CPH, (h + 1) * CPH):
                            if t == half == 0 and c % 2 == 0:
                                pe.wait_ge(sem("u_ready"), c // 2 + 1)
                            u = IC + c // 2
                            w = slot(u % RING).rearrange("p (c n) -> p c n", c=2)
                            last = mm(bank[LN.mlstm[t][half]][:, :], M.zT[:, c, t * P:(t + 1) * P],
                                      w[:, c % 2, half * 512:half * 512 + 512], start=(c == 0), stop=(c == IC - 1),
                                      skip_group_check=True)
                            if (t, half) == (TC - 1, 1) and c % 2 and c < IC - 1:
                                last.then_inc(sem("out_used"), 1)
                        if h == M_HEADS - 1:
                            last.then_inc(sem("y_ready"), 1)

            head(0)
            z(12)
            z(13)
            turn(0, 0)
            head(1)
            turn(0, 1)
            z(14)
            z(15)
            turn(1, 0)
            head(2)
            turn(1, 1)
            way_out(0)
            turn(2, 0)
            head(3)
            turn(2, 1)
            way_out(1)
            turn(3, 0)
            turn(3, 1)
            way_out(2)
            way_out(3)
            moe(1)

def build(nc, shapes):
    a = {name: nc.dram_tensor(f"in_{name}", shape, dt, kind="ExternalInput").ap()
         for name, (shape, dt) in shapes.items()}
    out = nc.dram_tensor("out", (S, D), F32, kind="ExternalOutput").ap()
    build_trunk(nc, a, out)

def kernel(**inputs):
    import numpy as np
    from concourse import bacc
    from concourse.bass_utils import run_bass_kernel_spmd

    def get(name):
        return np.asarray(inputs[name])

    def columns(v):
        return v.reshape(-1, P).T

    arrays = {}
    x = get("x")[0]
    arrays["x"] = x
    arrays["xT"] = x.T.reshape(DC, P, S).transpose(1, 0, 2)
    arrays["positions"] = get("positions").reshape(S)
    arrays["mla_in"] = get("mla_w_in")[0].reshape(DC, P, 576).transpose(1, 0, 2)
    uq = get("mla_w_uq")[0].reshape(RC, P, HEADS, P + ROPE)
    rope = uq[..., P:].reshape(RC, P, HEADS // HEADS_PER_ROPE, HEADS_PER_ROPE, 2, HALF).transpose(0, 1, 2, 4, 3, 5)
    arrays["mla_uq"] = np.concatenate([uq[..., :P].reshape(RC, P, -1), rope.reshape(RC, P, -1)], -1).transpose(1, 0, 2)
    ukv = get("mla_w_ukv")[0].reshape(RC, P, HEADS, 2, P).transpose(1, 0, 3, 2, 4)
    arrays["mla_ukv"] = ukv.reshape(P, RC, 2048)
    arrays["mla_o"] = get("mla_w_o")[0].reshape(HEADS, P, D).transpose(1, 0, 2)
    inv_freq = np.float32(1) / np.float32(10000) ** (np.arange(0, ROPE, 2, dtype=np.float32) / np.float32(ROPE))
    arrays["cols"] = np.concatenate([
        columns(get("mla_g_q")[0]), columns(get("mla_g_kv")[0]),
        get("mlstm_conv_w")[0].reshape(TAPS, IC, P).transpose(2, 1, 0).reshape(P, -1),
        columns(get("mlstm_conv_b")[0]), columns(get("mlstm_g_out")[0]), columns(get("mlstm_skip")[0]),
        np.tile(inv_freq, P // HALF)[:, None]], 1)
    arrays["ln"] = np.stack([get("ln_g"), get("ln_b")], 2).reshape(4, 2, D)
    arrays["router_w"] = get("router_w").reshape(DC, P, EXPERTS).transpose(1, 0, 2)
    arrays["router_b"] = get("router_b")
    arrays["gate_b"] = np.concatenate([get("mlstm_b_ig")[0], get("mlstm_b_fg")[0]])
    arrays["gate_w"] = np.concatenate([get("mlstm_w_ig")[0], get("mlstm_w_fg")[0]], -1
                                        ).reshape(3, IC, P // BLK, BLK, 2 * M_HEADS
                                                  ).transpose(2, 0, 1, 3, 4).repeat(BLK, 0)
    arrays["w_blocks"] = np.stack([get(f"mlstm_w_{n}")[0].reshape(IC, P, BLK).transpose(1, 0, 2) for n in "qkv"], 1)
    up = np.stack([get("moe_w_gate"), get("moe_w_up")]).reshape(2, 2, PAIRS, 2, DC, P, FF)
    up = up.transpose(1, 2, 4, 5, 0, 3, 6).reshape(2, PAIRS, DC, P, UNIT)
    down = get("moe_w_down").reshape(2, PAIRS, 2, 2, 2, P, 2, 512)
    down = down.transpose(0, 1, 6, 3, 5, 4, 2, 7).reshape(2, PAIRS, 4, P, UNIT)
    arrays["moe"] = np.concatenate([up, down], 2)
    m_in = get("mlstm_w_in")[0].reshape(DC, P, IC, 2, P).transpose(2, 1, 3, 0, 4).reshape(IC, P, UNIT)
    m_out = get("mlstm_w_out")[0].reshape(IC // 2, 2, P, D).transpose(0, 2, 1, 3).reshape(IC // 2, P, UNIT)
    arrays["mlstm"] = np.concatenate([m_in, m_out], 0)
    arrays = {n: np.ascontiguousarray(v) for n, v in arrays.items()}

    nc = bacc.Bacc("TRN2", target_bir_lowering=False, num_devices=1)
    build(nc, {n: (v.shape, mybir.dt.from_np(v.dtype)) for n, v in arrays.items()})
    result = run_bass_kernel_spmd(nc, [{f"in_{n}": v for n, v in arrays.items()}], core_ids=[0])
    return result.results[0]["out"].reshape(1, S, D)
```
